# Optimizing a Trainium2 kernel written in Bass

```python
import math
import jax, jax.numpy as jnp
from jax import lax
import numpy as np

D_MODEL = 1024
BATCH = 1
SEQ = 256
DEPTH = 1

HEAD_DIM = 64
N_HEADS_MIX = 8
BRANCH_WIDTH = N_HEADS_MIX * HEAD_DIM
N_BRANCHES = 3
IDX_HEADS = 16
IDX_DIM = 64
TOPK_MAX = 256
Q_BLOCK = 128
D_FF = 4 * D_MODEL
LN_EPS = 1e-5
DEEPNORM_ALPHA = (2.0 * DEPTH) ** 0.25
DEEPNORM_BETA = (8.0 * DEPTH) ** -0.25
FORGET_BIAS_MEAN = 3.0

IN_SIZES = (
    BRANCH_WIDTH, BRANCH_WIDTH, BRANCH_WIDTH,
    IDX_HEADS * IDX_DIM, IDX_DIM, IDX_HEADS,
    BRANCH_WIDTH, BRANCH_WIDTH, BRANCH_WIDTH,
    N_HEADS_MIX,
    BRANCH_WIDTH, BRANCH_WIDTH, BRANCH_WIDTH,
    N_BRANCHES * D_MODEL,
)
V_SECTIONS = (2, 8, 12)
IN_COLS = sum(IN_SIZES)


def _layer_norm(x, g, b):
    xf = x.astype(jnp.float32)
    mu = jnp.mean(xf, axis=-1, keepdims=True)
    xc = xf - mu
    var = jnp.mean(xc * xc, axis=-1, keepdims=True)
    y = xc * lax.rsqrt(var + LN_EPS) * g.astype(jnp.float32) + b.astype(jnp.float32)
    return y.astype(x.dtype)

def _alibi_slopes(n):
    return 2.0 ** (-8.0 * jnp.arange(1, n + 1, dtype=jnp.float32) / n)

def _to_blocks(a):
    b, s = a.shape[:2]
    a = a.reshape((b, s // Q_BLOCK, Q_BLOCK) + a.shape[2:])
    return jnp.moveaxis(a, 1, 0)

def _from_blocks(a):
    a = jnp.moveaxis(a, 0, 1)
    b, nb, qb = a.shape[:3]
    return a.reshape(b, nb * qb, -1)

def _dsa_attention(q, k, v, q_idx, k_idx, w_idx, slopes):
    s_len = q.shape[1]
    topk = min(TOPK_MAX, s_len // 4)
    pos = jnp.arange(s_len)
    scale = HEAD_DIM ** -0.5

    def block(args):
        qb, qib, wb, tq = args
        dots = jnp.einsum('bqhd,bkd->bqhk', qib, k_idx, preferred_element_type=jnp.float32)
        score = jnp.einsum('bqhk,bqh->bqk', jax.nn.relu(dots), wb.astype(jnp.float32))
        causal = pos[None, :] <= tq[:, None]
        score = jnp.where(causal[None], score, -jnp.inf)
        _, idx = lax.top_k(score, topk)
        valid = idx <= tq[None, :, None]
        k_sel = jax.vmap(lambda kb, ib: kb[ib])(k, idx)
        v_sel = jax.vmap(lambda vb, ib: vb[ib])(v, idx)
        logits = jnp.einsum('bqhd,bqkhd->bhqk', qb, k_sel, preferred_element_type=jnp.float32) * scale
        dist = (tq[None, :, None] - idx).astype(jnp.float32)
        logits = logits - slopes[None, :, None, None] * dist[:, None]
        logits = jnp.where(valid[:, None], logits, -jnp.inf)
        p = jax.nn.softmax(logits, axis=-1).astype(v.dtype)
        return jnp.einsum('bhqk,bqkhd->bqhd', p, v_sel)

    out = lax.map(block, (_to_blocks(q), _to_blocks(q_idx), _to_blocks(w_idx), pos.reshape(-1, Q_BLOCK)))
    return _from_blocks(out)

def _forgetting_attention(q, k, v, log_f):
    s_len = q.shape[1]
    pos = jnp.arange(s_len)
    scale = HEAD_DIM ** -0.5
    c = jnp.cumsum(log_f, axis=1)
    c_k = jnp.transpose(c, (0, 2, 1))[:, :, None, :]

    def block(args):
        qb, cq, tq = args
        logits = jnp.einsum('bqhd,bkhd->bhqk', qb, k, preferred_element_type=jnp.float32) * scale
        logits = logits + jnp.transpose(cq, (0, 2, 1))[..., None] - c_k
        causal = pos[None, :] <= tq[:, None]
        logits = jnp.where(causal[None, None], logits, -jnp.inf)
        p = jax.nn.softmax(logits, axis=-1).astype(v.dtype)
        return jnp.einsum('bhqk,bkhd->bqhd', p, v)

    out = lax.map(block, (_to_blocks(q), _to_blocks(c), pos.reshape(-1, Q_BLOCK)))
    return _from_blocks(out)

def _stick_breaking_attention(q, k, v):
    s_len = q.shape[1]
    pos = jnp.arange(s_len)
    scale = HEAD_DIM ** -0.5

    def block(args):
        qb, tq = args
        z = jnp.einsum('bqhd,bkhd->bhqk', qb, k, preferred_element_type=jnp.float32) * scale
        strict = (pos[None, :] < tq[:, None])[None, None]
        log_beta = jax.nn.log_sigmoid(z)
        log_one_minus = jnp.where(strict, jax.nn.log_sigmoid(-z), 0.0)
        later = lax.cumsum(log_one_minus, axis=3, reverse=True) - log_one_minus
        a = jnp.where(strict, jnp.exp(log_beta + later), 0.0).astype(v.dtype)
        return jnp.einsum('bhqk,bkhd->bqhd', a, v)

    out = lax.map(block, (_to_blocks(q), pos.reshape(-1, Q_BLOCK)))
    return _from_blocks(out)

def first_inputs(seed: int = 0) -> dict:
    key = jax.random.key(seed)
    ks = jax.random.split(key, 12)
    x = jax.random.normal(ks[0], (BATCH, SEQ, D_MODEL), jnp.float32)
    sec_keys = jax.random.split(ks[1], len(IN_SIZES))
    secs = []
    for i, size in enumerate(IN_SIZES):
        sc = D_MODEL ** -0.5 * (DEEPNORM_BETA if i in V_SECTIONS else 1.0)
        secs.append(jax.random.normal(sec_keys[i], (DEPTH, D_MODEL, size), jnp.float32) * sc)
    w_in = jnp.concatenate(secs, axis=-1)
    b_forget = FORGET_BIAS_MEAN + 0.5 * jax.random.normal(ks[2], (DEPTH, N_HEADS_MIX), jnp.float32)
    w_branch = jax.random.normal(ks[3], (DEPTH, N_BRANCHES, BRANCH_WIDTH, D_MODEL), jnp.float32) * (BRANCH_WIDTH ** -0.5 * DEEPNORM_BETA)
    w_out = jax.random.normal(ks[4], (DEPTH, D_MODEL, D_MODEL), jnp.float32) * (D_MODEL ** -0.5 * DEEPNORM_BETA)
    ln1_g = 1.0 + 0.05 * jax.random.normal(ks[5], (DEPTH, D_MODEL), jnp.float32)
    ln1_b = 0.02 * jax.random.normal(ks[6], (DEPTH, D_MODEL), jnp.float32)
    w_ff1 = jax.random.normal(ks[7], (DEPTH, D_MODEL, D_FF), jnp.float32) * (D_MODEL ** -0.5 * DEEPNORM_BETA)
    w_ff2 = jax.random.normal(ks[8], (DEPTH, D_FF, D_MODEL), jnp.float32) * (D_FF ** -0.5 * DEEPNORM_BETA)
    ln2_g = 1.0 + 0.05 * jax.random.normal(ks[9], (DEPTH, D_MODEL), jnp.float32)
    ln2_b = 0.02 * jax.random.normal(ks[10], (DEPTH, D_MODEL), jnp.float32)
    return {'x': x, 'w_in': w_in, 'b_forget': b_forget, 'w_branch': w_branch, 'w_out': w_out,
            'ln1_g': ln1_g, 'ln1_b': ln1_b, 'w_ff1': w_ff1, 'w_ff2': w_ff2,
            'ln2_g': ln2_g, 'ln2_b': ln2_b}

def first_block(x, w_in, b_forget, w_branch, w_out, ln1_g, ln1_b, w_ff1, w_ff2, ln2_g, ln2_b):
    b, s, _ = x.shape
    slopes = _alibi_slopes(N_HEADS_MIX)
    split_at = [int(v) for v in np.cumsum(IN_SIZES)[:-1]]

    def heads(a):
        return a.reshape(b, s, N_HEADS_MIX, HEAD_DIM)

    for layer in range(DEPTH):
        proj = jnp.einsum('bsd,dc->bsc', x, w_in[layer])
        (qa, ka, va, qi, ki, wi, qf, kf, vf, fg, qs, ks_, vs, gates) = jnp.split(proj, split_at, axis=-1)
        o_a = _dsa_attention(heads(qa), heads(ka), heads(va),
                             qi.reshape(b, s, IDX_HEADS, IDX_DIM), ki, wi, slopes)
        log_f = jax.nn.log_sigmoid((fg + b_forget[layer]).astype(jnp.float32))
        o_b = _forgetting_attention(heads(qf), heads(kf), heads(vf), log_f)
        o_c = _stick_breaking_attention(heads(qs), heads(ks_), heads(vs))
        branches = jnp.stack([o_a, o_b, o_c], axis=0)
        up = jnp.einsum('ibsw,iwd->bsid', branches, w_branch[layer])
        g = jax.nn.sigmoid(gates.reshape(b, s, N_BRANCHES, D_MODEL))
        merged = jnp.sum(up * g, axis=2)
        y = jnp.einsum('bsd,de->bse', merged, w_out[layer])
        x = _layer_norm(DEEPNORM_ALPHA * x + y, ln1_g[layer], ln1_b[layer])
        h = jnp.square(jax.nn.relu(jnp.einsum('bsd,df->bsf', x, w_ff1[layer])))
        y = jnp.einsum('bsf,fd->bsd', h, w_ff2[layer])
        x = _layer_norm(DEEPNORM_ALPHA * x + y, ln2_g[layer], ln2_b[layer])
    return x


CHUNK = 64
EPS = 1e-6
HG_HEADS = 8
HG_DK = 128
HG_DV = D_MODEL // HG_HEADS
HG_WIDTH_K = HG_HEADS * HG_DK
HG_WIDTH_V = HG_HEADS * HG_DV
GDN_QK_HEADS = 8
GDN_V_HEADS = 16
GDN_DK = 128
GDN_DV = 128
GDN_WIDTH_K = GDN_QK_HEADS * GDN_DK
GDN_WIDTH_V = GDN_V_HEADS * GDN_DV
CONV_K = 4
D_FF_2 = 2816
IN_SIZES_2 = (HG_WIDTH_K, HG_WIDTH_K, HG_WIDTH_V, HG_WIDTH_V,
            GDN_WIDTH_K, GDN_WIDTH_K, GDN_WIDTH_V, GDN_V_HEADS, GDN_V_HEADS, GDN_WIDTH_V,
            D_MODEL, D_MODEL)
IN_WIDTH = sum(IN_SIZES_2)


def rmsnorm(x, g):
    xf = x.astype(jnp.float32)
    y = xf * lax.rsqrt(jnp.mean(xf * xf, axis=-1, keepdims=True) + EPS)
    return (y * g).astype(x.dtype)

def l2norm(x):
    return x * lax.rsqrt(jnp.sum(x * x, axis=-1, keepdims=True) + EPS)

def swiglu(x, w_in, w_out):
    a, b = jnp.split(x @ w_in, 2, axis=-1)
    return (jax.nn.silu(a) * b) @ w_out

def to_chunks(t, n_heads):
    B, S = t.shape[:2]
    t = t.reshape(B, S // CHUNK, CHUNK, n_heads, -1)
    return jnp.transpose(t, (0, 3, 1, 2, 4))

def from_chunks(t):
    B, H, NC, C, d = t.shape
    return jnp.transpose(t, (0, 2, 3, 1, 4)).reshape(B, NC * C, H, d)

def causal_short_conv(x, w):
    K = w.shape[0]
    S = x.shape[1]
    xp = jnp.pad(x, ((0, 0), (K - 1, 0), (0, 0)))
    return sum(xp[:, j:j + S] * w[j] for j in range(K))

def hgrn2_chunked(q, k, v, log_f):
    B, H, NC, C, DK = q.shape
    DV = v.shape[-1]
    b_cum = jnp.cumsum(log_f, axis=3)
    causal = jnp.tril(jnp.ones((C, C), dtype=bool))[:, :, None]

    def step(S, inp):
        q_c, k_c, v_c, b_c = inp
        inter = jnp.einsum('bhtk,bhkv->bhtv', q_c * jnp.exp(b_c), S)
        diff = b_c[:, :, :, None, :] - b_c[:, :, None, :, :]
        decay = jnp.exp(jnp.where(causal, diff, -jnp.inf))
        scores = jnp.einsum('bhtk,bhsk,bhtsk->bhts', q_c, k_c, decay)
        intra = jnp.einsum('bhts,bhsv->bhtv', scores, v_c)
        b_end = b_c[:, :, -1, :]
        k_to_end = k_c * jnp.exp(b_end[:, :, None, :] - b_c)
        S = jnp.exp(b_end)[..., None] * S + jnp.einsum('bhsk,bhsv->bhkv', k_to_end, v_c)
        return S, inter + intra

    S0 = jnp.zeros((B, H, DK, DV), jnp.float32)
    xs = (jnp.moveaxis(q, 2, 0), jnp.moveaxis(k, 2, 0), jnp.moveaxis(v, 2, 0), jnp.moveaxis(b_cum, 2, 0))
    _, o = lax.scan(step, S0, xs)
    return jnp.moveaxis(o, 0, 2)

def gated_delta_chunked(q, k, v, beta, g):
    B, H, NC, C, DK = q.shape
    DV = v.shape[-1]
    gam = jnp.cumsum(g, axis=-1)
    incl = jnp.tril(jnp.ones((C, C), dtype=bool))
    strict = jnp.tril(jnp.ones((C, C), dtype=bool), -1)
    diff = gam[..., :, None] - gam[..., None, :]
    Lmat = jnp.exp(jnp.where(incl, diff, -jnp.inf))
    kb = k * beta[..., None]
    A = jnp.where(strict, jnp.einsum('bhntk,bhnsk->bhnts', kb, k) * Lmat, 0.0)
    eye = jnp.eye(C, dtype=A.dtype)
    T = lax.linalg.triangular_solve(eye + A, jnp.broadcast_to(eye, A.shape),
                                    left_side=True, lower=True, unit_diagonal=True)
    u = jnp.matmul(T, v * beta[..., None])
    w = jnp.matmul(T, kb * jnp.exp(gam)[..., None])
    qk = jnp.einsum('bhntk,bhnsk->bhnts', q, k) * Lmat

    def step(S, inp):
        q_c, k_c, u_c, w_c, qk_c, gam_c = inp
        v_new = u_c - jnp.einsum('bhtk,bhkv->bhtv', w_c, S)
        o = (jnp.einsum('bhtk,bhkv->bhtv', q_c * jnp.exp(gam_c)[..., None], S)
             + jnp.einsum('bhts,bhsv->bhtv', qk_c, v_new))
        g_end = gam_c[..., -1]
        k_to_end = k_c * jnp.exp(g_end[..., None] - gam_c)[..., None]
        S = S * jnp.exp(g_end)[..., None, None] + jnp.einsum('bhsk,bhsv->bhkv', k_to_end, v_new)
        return S, o

    S0 = jnp.zeros((B, H, DK, DV), jnp.float32)
    xs = tuple(jnp.moveaxis(t, 2, 0) for t in (q, k, u, w, qk, gam))
    _, o = lax.scan(step, S0, xs)
    return jnp.moveaxis(o, 0, 2)

def hybrid_mixer(u, w_in, lb, hgrn_out_norm, conv_w, a_log, dt_bias, gdn_out_norm,
                 w_branch_hgrn, w_branch_gdn, w_out):
    B, S, _ = u.shape
    f32 = jnp.float32
    proj = (u @ w_in).astype(f32)
    offsets = np.cumsum(IN_SIZES_2)[:-1].tolist()
    (hq, hf, hi, hg, gq, gk, gv, ga, gb, gz, gate_h, gate_g) = jnp.split(proj, offsets, axis=-1)

    lb = lb.astype(f32)
    log_f = jnp.logaddexp(jnp.log(lb), jnp.log1p(-lb) + jax.nn.log_sigmoid(hf))
    k_h = -jnp.expm1(log_f)
    q_h = jax.nn.silu(hq) * HG_DK ** -0.5
    o_h = hgrn2_chunked(to_chunks(q_h, HG_HEADS), to_chunks(k_h, HG_HEADS),
                        to_chunks(hi, HG_HEADS), to_chunks(log_f, HG_HEADS))
    o_h = rmsnorm(from_chunks(o_h), hgrn_out_norm) * jax.nn.silu(hg).reshape(B, S, HG_HEADS, HG_DV)
    y_h = o_h.reshape(B, S, HG_WIDTH_V) @ w_branch_hgrn

    qkv = jax.nn.silu(causal_short_conv(jnp.concatenate([gq, gk, gv], axis=-1), conv_w))
    cq, ck, cv = jnp.split(qkv, [GDN_WIDTH_K, 2 * GDN_WIDTH_K], axis=-1)
    rep = GDN_V_HEADS // GDN_QK_HEADS
    q_g = l2norm(cq.reshape(B, S, GDN_QK_HEADS, GDN_DK)) * GDN_DK ** -0.5
    k_g = l2norm(ck.reshape(B, S, GDN_QK_HEADS, GDN_DK))
    q_g = jnp.repeat(q_g, rep, axis=2).reshape(B, S, GDN_V_HEADS * GDN_DK)
    k_g = jnp.repeat(k_g, rep, axis=2).reshape(B, S, GDN_V_HEADS * GDN_DK)
    beta = jax.nn.sigmoid(gb)
    g = -jnp.exp(a_log.astype(f32)) * jax.nn.softplus(ga + dt_bias)
    o_g = gated_delta_chunked(to_chunks(q_g, GDN_V_HEADS), to_chunks(k_g, GDN_V_HEADS),
                              to_chunks(cv, GDN_V_HEADS),
                              to_chunks(beta[..., None], GDN_V_HEADS)[..., 0],
                              to_chunks(g[..., None], GDN_V_HEADS)[..., 0])
    o_g = rmsnorm(from_chunks(o_g), gdn_out_norm) * jax.nn.silu(gz).reshape(B, S, GDN_V_HEADS, GDN_DV)
    y_g = o_g.reshape(B, S, GDN_WIDTH_V) @ w_branch_gdn

    y = jax.nn.sigmoid(gate_h) * y_h + jax.nn.sigmoid(gate_g) * y_g
    return (y @ w_out).astype(u.dtype)

def second_inputs(seed: int = 0) -> dict:
    key = jax.random.key(seed)
    ks = jax.random.split(key, 20)
    f32 = jnp.float32
    L = DEPTH

    def dense(k, shape):
        return jax.random.normal(k, shape, f32) * shape[-2] ** -0.5

    def gain(k, shape):
        return 1.0 + 0.05 * jax.random.normal(k, shape, f32)

    A = jax.random.uniform(ks[8], (L, GDN_V_HEADS), f32, 1.0, 16.0)
    dt = jnp.exp(jax.random.uniform(ks[9], (L, GDN_V_HEADS), f32, math.log(1e-3), math.log(1e-1)))
    dt_bias = dt + jnp.log(-jnp.expm1(-dt))
    return {
        "x": jax.random.normal(ks[0], (BATCH, SEQ, D_MODEL), f32),
        "ffn1_norm": gain(ks[1], (L, D_MODEL)),
        "ffn1_w_in": dense(ks[2], (L, D_MODEL, 2 * D_FF_2)),
        "ffn1_w_out": dense(ks[3], (L, D_FF_2, D_MODEL)),
        "mix_norm": gain(ks[4], (L, D_MODEL)),
        "w_in": dense(ks[5], (L, D_MODEL, IN_WIDTH)),
        "hgrn_lb_logits": 0.5 * jax.random.normal(ks[6], (L + 1, HG_WIDTH_K), f32),
        "hgrn_out_norm": gain(ks[7], (L, HG_DV)),
        "gdn_conv_w": 0.5 * jax.random.normal(ks[10], (L, CONV_K, 2 * GDN_WIDTH_K + GDN_WIDTH_V), f32),
        "gdn_a_log": jnp.log(A),
        "gdn_dt_bias": dt_bias,
        "gdn_out_norm": gain(ks[11], (L, GDN_DV)),
        "w_branch_hgrn": dense(ks[12], (L, HG_WIDTH_V, D_MODEL)),
        "w_branch_gdn": dense(ks[13], (L, GDN_WIDTH_V, D_MODEL)),
        "w_out": dense(ks[14], (L, D_MODEL, D_MODEL)),
        "ffn2_norm": gain(ks[15], (L, D_MODEL)),
        "ffn2_w_in": dense(ks[16], (L, D_MODEL, 2 * D_FF_2)),
        "ffn2_w_out": dense(ks[17], (L, D_FF_2, D_MODEL)),
        "final_norm": gain(ks[18], (D_MODEL,)),
    }

def second_block(x, ffn1_norm, ffn1_w_in, ffn1_w_out, mix_norm, w_in, hgrn_lb_logits,
              hgrn_out_norm, gdn_conv_w, gdn_a_log, gdn_dt_bias, gdn_out_norm,
              w_branch_hgrn, w_branch_gdn, w_out, ffn2_norm, ffn2_w_in, ffn2_w_out,
              final_norm):
    lb_all = jnp.cumsum(jax.nn.softmax(hgrn_lb_logits.astype(jnp.float32), axis=0), axis=0)
    h = x
    for l in range(DEPTH):
        h = h + 0.5 * swiglu(rmsnorm(h, ffn1_norm[l]), ffn1_w_in[l], ffn1_w_out[l])
        h = h + hybrid_mixer(rmsnorm(h, mix_norm[l]), w_in[l], lb_all[l], hgrn_out_norm[l],
                             gdn_conv_w[l], gdn_a_log[l], gdn_dt_bias[l], gdn_out_norm[l],
                             w_branch_hgrn[l], w_branch_gdn[l], w_out[l])
        h = h + 0.5 * swiglu(rmsnorm(h, ffn2_norm[l]), ffn2_w_in[l], ffn2_w_out[l])
    return rmsnorm(h, final_norm)


def setup_inputs(seed=0):
    out = dict(first_inputs(seed))
    for name, value in second_inputs(seed + 1).items():
        if name != "x":
            out[name + "_2"] = value
    return out


def reference(
    x, w_in, b_forget, w_branch, w_out, ln1_g, ln1_b, w_ff1, w_ff2, ln2_g, ln2_b, ffn1_norm_2,
    ffn1_w_in_2, ffn1_w_out_2, mix_norm_2, w_in_2, hgrn_lb_logits_2, hgrn_out_norm_2,
    gdn_conv_w_2, gdn_a_log_2, gdn_dt_bias_2, gdn_out_norm_2, w_branch_hgrn_2, w_branch_gdn_2,
    w_out_2, ffn2_norm_2, ffn2_w_in_2, ffn2_w_out_2, final_norm_2,
):
    x = first_block(
        x, w_in, b_forget, w_branch, w_out, ln1_g, ln1_b, w_ff1, w_ff2, ln2_g, ln2_b,
    )
    return second_block(
        x, ffn1_norm_2, ffn1_w_in_2, ffn1_w_out_2, mix_norm_2, w_in_2, hgrn_lb_logits_2,
        hgrn_out_norm_2, gdn_conv_w_2, gdn_a_log_2, gdn_dt_bias_2, gdn_out_norm_2,
        w_branch_hgrn_2, w_branch_gdn_2, w_out_2, ffn2_norm_2, ffn2_w_in_2, ffn2_w_out_2,
        final_norm_2,
    )


_drawn_inputs = setup_inputs


def setup_inputs(seed=0):
    import zlib

    import numpy as np

    out = dict(_drawn_inputs(seed))
    spreads = {}
    factors = {'b_forget': 59.528,
     'hgrn_lb_logits_2': 3.314,
     'hgrn_out_norm_2': 4.25,
     'gdn_out_norm_2': 3.673,
     'ffn2_norm_2': 3.152}
    for name, (base, spread) in spreads.items():
        noise = np.random.default_rng([zlib.crc32(name.encode()), seed]).standard_normal(out[name].shape)
        drawn = base * np.exp(spread * noise) if base else spread * noise
        out[name] = __import__('jax').numpy.asarray(drawn.astype(out[name].dtype))
    for name, factor in factors.items():
        out[name] = (out[name] * factor).astype(out[name].dtype)
    return out
```

```python
from contextlib import ExitStack

import concourse.bass as bass
from concourse import mybir

ALU = mybir.AluOpType
ACT = mybir.ActivationFunctionType
AX_X = mybir.AxisListType.X
F32 = mybir.dt.float32
F32R = mybir.dt.float32r
I32 = mybir.dt.int32
ds = bass.ds

P = 128
T = 256
TT = T // P
D = 1024
KT = D // P
HD = 64
NH = 8
BW = NH * HD
PAIRS = NH // 2
IDXH = 16
TOPK = 64
FF = 4 * D
FF2 = 2816
CW = 256
CHUNK = KT * CW
RING = 3
ALPHA = 2.0 ** 0.25
LN_EPS = 1e-5
RMS_EPS = 1e-6
NEG = -1e30
TAKEN = -3e38

SIZES = (BW, BW, BW, IDXH * HD, HD, IDXH, BW, BW, BW, NH, BW, BW, BW, 3 * D)
(O_QA, O_KA, O_VA, O_QI, O_KI, O_WI, O_QF, O_KF, O_VF, O_FG, O_QS, O_KS, O_VS, O_G) = [
    sum(SIZES[:i]) for i in range(len(SIZES))]

WK = 1024
GH = 8
VH = 2 * GH
SIZES2 = (WK, WK, WK, WK, WK, WK, 2 * WK, VH, VH, 2 * WK, D, D)
(O_HQ, O_HF, O_HI, O_HG, O_GQ, O_GK, O_GV, O_GA, O_GB, O_GZ, O_GTH, O_GTG) = [
    sum(SIZES2[:i]) for i in range(len(SIZES2))]
QSCALE = 128 ** -0.5
CONV = 4
LEVELS = 7

SECTIONS = (("small", 1), ("qi", 4), ("va", 2), ("gates", 4), ("pairs", 6 * PAIRS), ("branch", 6),
            ("wout", 4), ("ff", 32), ("ffn1", 33), ("ba", 1), ("heads", 48), ("yh", 4), ("yg", 8),
            ("wout2", 4), ("ffn2", 33))
FIRST = {name: sum(n for _, n in SECTIONS[:i]) for i, (name, _) in enumerate(SECTIONS)}
CHUNKS = sum(n for _, n in SECTIONS)
EV_FF = ((FIRST["branch"] + 1) // 2, FIRST["branch"] // 2, 0)
STEPS = FF2 // P
EV_FFN1 = (EV_FF[0] + 6, EV_FF[1] + 5)
EV_BA = EV_FFN1[0] + STEPS // 2
EV_HEADS = (EV_BA + 1, EV_FFN1[1] + STEPS // 2)
EV_Y = (EV_HEADS[0] + 3 * GH, EV_HEADS[1] + 3 * GH)
EV_FFN2 = (EV_Y[0] + 6, EV_Y[1] + 6)
H_FFN1 = FF // CW
H_FFN2 = H_FFN1 + STEPS
V_FFN1, V_MIX, V_FFN2, V_LB0, V_LB1, V_HN, V_GN = 0, 8, 16, 24, 32, 40, 41
VECS = 42


def build_program(nc, a, out):
    with ExitStack() as ctx:
        emit(nc, ctx, a, out)


def emit(nc, ctx, a, out):
    def sb(name, shape, dt=F32):
        return ctx.enter_context(nc.sbuf_tensor(name, shape, dt))

    def sem(name):
        return ctx.enter_context(nc.semaphore(name))

    w_raw = sb("w_raw", [P, RING, CHUNK])
    w_hi = sb("w_hi", [P, RING, CHUNK], F32R)
    w_lo = sb("w_lo", [P, RING, CHUNK], F32R)
    xa_hi = sb("xa_hi", [P, KT, T], F32R)
    xa_lo = sb("xa_lo", [P, KT, T], F32R)
    xb_hi = sb("xb_hi", [P, 16, T], F32R)
    xb_lo = sb("xb_lo", [P, 16, T], F32R)
    res = sb("res", [P, TT, D])
    ident = sb("ident", [P, P])
    ones = sb("ones", [P, P])
    tri = sb("tri", [P, P])
    below = sb("below", [P, P])
    lmask = sb("lmask", [P, 7, P])
    lmask_t = sb("lmask_t", [P, 7, P])
    eps = sb("eps", [P, 2])
    stat = sb("stat", [P, 64])
    ARENA = 17800
    arena = sb("arena", [P, ARENA])

    class Carver:
        def __init__(self):
            self.at = 0

        def __call__(self, n):
            self.at += n
            assert self.at <= ARENA, self.at
            return arena[:, self.at - n:self.at]

    def grid(ap, **sizes):
        names = " ".join(sizes)
        return ap.rearrange(f"p ({names}) -> p {names}", **sizes)

    carve = Carver()
    gates = grid(carve(24 * T), n=24, t=T)
    dist = carve(3 * P)
    caus = carve(3 * P)
    strict = carve(3 * P)
    slopes = carve(NH)
    ki_t = carve(T)
    wi = grid(carve(TT * 24), i=TT, h=24)
    bfor = carve(NH)
    fgx = grid(carve(TT * NH), i=TT, h=NH)
    fgn = grid(carve(TT * NH), i=TT, h=NH)
    log_f = grid(carve(TT * NH), i=TT, h=NH)
    c_f = grid(carve(TT * NH), i=TT, h=NH)
    score = carve(3 * P)
    selb = carve(3 * P)
    top8 = grid(carve(16), i=2, n=8)
    qs_t, ks_t, qa_t, ka_t, qf_t, kf_t = (carve(T) for _ in range(6))
    vfs = grid(carve(TT * T), i=TT, c=T)
    va = grid(carve(TT * BW), i=TT, c=BW)
    va_p = grid(carve(TT * P), i=TT, c=P)
    log_a = grid(carve(6 * P), e=2, k=3 * P)
    pt_a = grid(carve(6 * P), e=2, k=3 * P)
    log_fo = grid(carve(6 * P), e=2, k=3 * P)
    pt_f = grid(carve(6 * P), e=2, k=3 * P)
    st1 = grid(carve(6 * P), e=2, k=3 * P)
    st2 = grid(carve(6 * P), e=2, k=3 * P)
    st3 = grid(carve(6 * P), e=2, k=3 * P)
    fbc = grid(carve(TT * 2 * P), i=TT, e=2, c=P)
    cq = grid(carve(TT * 2), i=TT, e=2)
    nmx = [grid(carve(4), i=2, e=2) for _ in range(2)]
    rsum = [grid(carve(4), i=2, e=2) for _ in range(2)]
    rinv = [grid(carve(4), i=2, e=2) for _ in range(2)]
    spare = Carver()
    spare.at = ARENA - 2560
    qi_t = grid(spare(1024), b=2, c=512)
    relu_d = grid(spare(1536), e=4, k=3 * P)
    late = Carver()
    late.at = 24 * T + 64
    rows = grid(late(2 * D), i=2, d=D)
    tmp = grid(late(2 * D), i=TT, d=D)
    ffr = grid(late(3 * 512), b=3, c=512)
    ffs = grid(late(3 * 512), b=3, c=512)
    mrg = late(1024)
    mrg2 = late(1024)
    vec_rows = late(P)
    conv_rows = late(P)
    keep = Carver()
    keep.at = ARENA - 320
    vec = keep(48)
    conv = grid(keep(P), j=CONV, n=32)
    ab2 = grid(keep(2 * VH), i=2, h=VH)
    lb = keep(GH)
    lb1 = keep(GH)
    ffn_s = grid(late(512), b=2, c=T)
    ffn_h = grid(late(512), b=2, c=T)
    late_end = late.at
    mix = Carver()
    gates2 = grid(mix(16 * T), n=GH, b=2, t=T)
    o_h = grid(mix(GH * T), n=GH, t=T)
    hq, hk, hf, hb = (mix(T) for _ in range(4))
    dd = grid(mix(2 * T), b=2, t=T)
    kqd = grid(mix(2 * T), b=2, t=T)
    eh = dd.rearrange("p b t -> p (b t)")
    hr = kqd.rearrange("p b t -> p (b t)")
    sct = mix(3 * P)
    hv = grid(mix(T), i=TT, c=P)
    hsg = mix(T)
    gbc_flat = mix(2 * T)
    hsq, hrs = gbc_flat[:, 0:T], gbc_flat[:, T:2 * T]
    gbc = grid(gbc_flat, i=TT, e=2, c=P)
    raw = grid(mix(4 * (T + 4)), n=4, t=T + 4)
    acc = grid(mix(4 * T), n=4, t=T)
    eg = mix(4 * T)
    cwt = grid(mix(4 * CONV), j=CONV, n=4)
    beta, nbeta = (grid(mix(TT * VH), i=TT, h=VH) for _ in range(2))
    gdec, gam = (grid(mix(TT * VH), i=TT, h=VH) for _ in range(2))
    gmx = mix(VH)
    abx = grid(mix(TT * 2 * VH), i=TT, h=2 * VH)
    abn = grid(mix(TT * VH), i=TT, h=VH)
    bst, nbst, gst = (grid(mix(4), i=TT, e=2) for _ in range(3))
    gmst = mix(2)
    vsd = grid(mix(4 * P), i=TT, e=2, c=P)
    lt = grid(mix(6 * P), e=2, k=3 * P)
    nt = grid(eg[:, 2 * T:4 * T], i=TT, e=2, c=P)
    mt = grid(mix(2 * P), e=2, c=P)
    xi = grid(mix(4 * P), i=TT, e=2, c=P)
    yi = grid(eg[:, 0:2 * T], i=TT, e=2, c=P)
    zi = grid(mix(4 * P), i=TT, e=2, c=P)
    vn0, r1, vn1 = vsd[:, 0], vsd[:, 1], vsd[:, 1]
    sgz = grid(mix(2 * T), e=2, t=T)
    sgz2 = grid(mix(2 * T), e=2, t=T)
    assert mix.at <= ARENA - 320 and late_end <= ARENA - 320, (mix.at, late_end)
    fin_row = rows[:, 0, :]

    G = ctx.enter_context(nc.psum_tensor("G", [P, 2, 512], F32))
    M = ctx.enter_context(nc.psum_tensor("M", [P, 6, 512], F32))

    def ffbank(r):
        return G[:, r, :] if r < 2 else M[:, 5, :]

    x_loaded = sem("x_loaded")
    par_loaded = sem("par_loaded")
    rows_loaded = sem("rows_loaded")
    w_loaded = [sem(f"w_loaded{s}") for s in range(RING)]
    slot_passed = sem("slot_passed")
    waited = sem("waited")
    hi_ready = sem("hi_ready")
    lo_ready = sem("lo_ready")
    gemm_done = sem("gemm_done")
    evac = [sem(f"evac{b}") for b in range(3)]
    built = sem("built")
    xt_done, xh_ready, xl_ready = sem("xt_done"), sem("xh_ready"), sem("xl_ready")
    dots_done, relu_ready, relu_used = sem("dots_done"), sem("relu_ready"), sem("relu_used")
    fg_ready, fln_ready, logf_ready, cum_done, c_ready = (
        sem(n) for n in ("fg_ready", "fln_ready", "logf_ready", "cum_done", "c_ready"))
    va_ready = sem("va_ready")
    fbc_ready, ck_done, mck_ready = sem("fbc_ready"), sem("ck_done"), sem("mck_ready")
    z_done, sp_ready, lom_ready, later_done, lb_ready, ex_ready, stick_ready = (
        sem(n) for n in ("z_done", "sp_ready", "lom_ready", "later_done", "lb_ready", "ex_ready", "stick_ready"))
    sc_done = [sem("sa_done"), sem("sf_done")]
    max_ready = [sem("maxa_ready"), sem("maxf_ready")]
    exp_ready = [sem("expa_ready"), sem("expf_ready")]
    prob_ready = [sem("proba_ready"), sem("probf_ready")]
    pt_done = [sem("pta_done"), sem("ptf_done")]
    pt_ready = [sem("pta_ready"), sem("ptf_ready")]
    o_done = [sem("oa_done"), sem("of_done"), sem("os_done")]
    oh_ready = [sem("oah_ready"), sem("ofh_ready"), sem("osh_ready")]
    ol_ready = [sem("oal_ready"), sem("ofl_ready"), sem("osl_ready")]
    branch_used, mrg_ready, mh_ready, ml_ready = (
        sem(n) for n in ("branch_used", "mrg_ready", "mh_ready", "ml_ready"))
    var_ready, rstd_ready, x_normed, y_used = (sem(n) for n in ("var_ready", "rstd_ready", "x_normed", "y_used"))
    ffr_ready, hh_ready, h_ready = (sem(n) for n in ("ffr_ready", "hh_ready", "h_ready"))
    stored = sem("stored")
    vecs_loaded, vec_done, vec_ready = (sem(n) for n in ("vecs_loaded", "vec_done", "vec_ready"))
    ab_ready, abln_ready, g_ready, gsum_done, lb_exp = (
        sem(n) for n in ("ab_ready", "abln_ready", "g_ready", "gsum_done", "lb_exp"))
    (hpv_done, hsq_ready, hss_done, hrs_ready, hfin, eh_ready, qk_ready, f_ready, lnf_ready, hgx_ready,
     dd_ready, lev_exp, wl_ready, lev_done, sc_used) = (sem(n) for n in (
        "hpv_done", "hsq_ready", "hss_done", "hrs_ready", "hfin", "eh_ready", "qk_ready", "f_ready", "lnf_ready",
        "hgx_ready", "dd_ready", "lev_exp", "wl_ready", "lev_done", "sc_used"))
    (conv_ready, ec_ready, act_ready, sq_ready, ss_done, rs_ready, vt_done, v_ready, gbc_ready, gam_done, lt_pre,
     lt_ready, qn_ready, kq_done, y0_ready, t_done, t_ready, zz_done, zc_ready, ww_done, xx_ready) = (sem(n) for n in (
        "conv_ready", "ec_ready", "act_ready", "sq_ready", "ss_done", "rs_ready", "vt_done", "v_ready", "gbc_ready",
        "gam_done", "lt_pre", "lt_ready", "qn_ready", "kq_done", "y0_ready", "t_done", "t_ready", "zz_done",
        "zc_ready", "ww_done", "xx_ready"))
    (vn0_done, vn0_ready, cross_done, r1_ready, vn1_done, vn1_ready, go_done, gsq_ready, gss_done, grs_ready,
     og_ready, ogh_ready, ogl_ready, sgz_moved, gzx_ready) = (sem(n) for n in (
        "vn0_done", "vn0_ready", "cross_done", "r1_ready", "vn1_done", "vn1_ready", "go_done", "gsq_ready",
        "gss_done", "grs_ready", "og_ready", "ogh_ready", "ogl_ready", "sgz_moved", "gzx_ready"))
    ohh_ready, ohl_ready, ym_ready, ymh_ready, yml_ready = (
        sem(n) for n in ("ohh_ready", "ohl_ready", "ym_ready", "ymh_ready", "yml_ready"))

    def after(engine, semaphore, count):
        if not (isinstance(count, int) and count <= 0):
            engine.wait_ge(semaphore, count)

    block = ctx.enter_context(nc.Block())

    w_in = a["w_in"][0].rearrange("(k p) c -> p k c", p=P)
    w_br = a["w_branch"][0].rearrange("i (k p) c -> i p k c", p=P)
    w_out = a["w_out"][0].rearrange("(k p) c -> p k c", p=P)
    w_f1 = a["w_ff1"][0].rearrange("(k p) c -> p k c", p=P)
    w_f2 = a["w_ff2"][0].rearrange("(k p) c -> p k c", p=P)
    w_up1, w_down1, w_in2, w_bh, w_bg, w_out2, w_up2, w_down2 = (
        a[name][0].rearrange("(k p) c -> p k c", p=P) for name in (
            "ffn1_w_in_2", "ffn1_w_out_2", "w_in_2", "w_branch_hgrn_2", "w_branch_gdn_2", "w_out_2",
            "ffn2_w_in_2", "ffn2_w_out_2"))

    def cols(ring, slot):
        return ring[:, slot, :].rearrange("p (k c) -> p k c", c=CW)

    def rows2(ring, slot):
        return ring[:, slot, :].rearrange("p (k c) -> p k c", c=D)

    @block.sync
    def _(sp):
        def slot_free(c):
            if isinstance(c, int) and c < RING:
                return
            sp.wait_ge(lo_ready, c - RING + 1)
            sp.sem_inc(slot_passed, 1)

        def load_cols(c, slot, w, col):
            slot_free(c)
            for k in (0, KT // 2):
                sp.dma_start(cols(w_raw, slot)[:, k:k + KT // 2, :], w[:, k:k + KT // 2, ds(col, CW)]
                             ).then_inc(w_loaded[slot], 16)

        def load_two(c, slot, w, col0, col1):
            slot_free(c)
            sp.dma_start(cols(w_raw, slot)[:, :, 0:P], w[:, :, ds(col0, P)]).then_inc(w_loaded[slot], 16)
            sp.dma_start(cols(w_raw, slot)[:, :, P:CW], w[:, :, ds(col1, P)]).then_inc(w_loaded[slot], 16)

        def load_rows(c, slot, w, k):
            slot_free(c)
            for j in range(2):
                sp.dma_start(rows2(w_raw, slot)[:, j:j + 1, :], w[:, ds(k + j, 1), :]).then_inc(w_loaded[slot], 16)

        x_in = a["x"][0].rearrange("(i p) d -> i p d", p=P)
        for i in range(TT):
            sp.dma_start(res[:, i, :], x_in[i]).then_inc(x_loaded, 16)
        small = cols(w_raw, 0)
        for lo_, col, n in ((0, O_KI, HD), (HD, O_KI, HD + IDXH), (P + IDXH, O_FG, NH), (P + IDXH + NH, 0, 104)):
            sp.dma_start(small[:, :, lo_:lo_ + n], w_in[:, :, col:col + n]).then_inc(w_loaded[0], 16)
        sp.dma_start(bfor, a["b_forget"][0].partition_broadcast(P)).then_inc(par_loaded, 16)
        for u in range(4):
            c = FIRST["qi"] + u
            load_cols(c, c % RING, w_in, O_QI + CW * u)
        for u in range(2):
            c = FIRST["va"] + u
            load_cols(c, c % RING, w_in, O_VA + CW * u)
        for u in range(4):
            c = FIRST["gates"] + u
            load_cols(c, c % RING, w_in, O_G + CW * u)
        c0 = FIRST["pairs"]
        with sp.Fori(0, PAIRS) as p:
            for j, (q, k) in enumerate(((O_QS, O_KS), (O_QA, O_KA), (O_QF, O_KF), (O_VF, O_VS))):
                load_two(c0 + j + p * 6, (c0 + j) % RING, w_in, q + p * P, k + p * P)
            for j in range(2):
                load_cols(c0 + 4 + j + p * 6, (c0 + 4 + j) % RING, w_in, O_G + CW * (4 + j) + p * (2 * CW))
        c0 = FIRST["branch"]
        with sp.Fori(0, 2) as half:
            for i in range(3):
                c = c0 + i + half * 3
                slot = (c0 + i) % RING
                slot_free(c)
                view = w_raw[:, slot, :].rearrange("p (k c) -> p k c", c=512)
                for k in (0, 2):
                    sp.dma_start(view[:, k:k + 2, :], w_br[i][:, k:k + 2, ds(half * 512, 512)]
                                 ).then_inc(w_loaded[slot], 16)
        for u in range(4):
            c = FIRST["wout"] + u
            load_rows(c, c % RING, w_out, 2 * u)
            if u == 0:
                sp.wait_ge(ol_ready[1], PAIRS)
                sp.wait_ge(ol_ready[2], PAIRS)
                for i, name in enumerate(("ln1_g", "ln1_b")):
                    sp.dma_start(rows[:, i, :], a[name][0].partition_broadcast(P)).then_inc(rows_loaded, 16)
                for at, name in ((V_FFN1, "ffn1_norm_2"), (V_MIX, "mix_norm_2"), (V_FFN2, "ffn2_norm_2")):
                    sp.dma_start(vec_rows[at:at + KT, :], a[name][0].rearrange("(k p) -> k p", p=P)
                                 ).then_inc(vecs_loaded, 16)
                sp.dma_start(vec_rows[V_LB0:V_LB0 + 2 * GH, :],
                             a["hgrn_lb_logits_2"].rearrange("l (k p) -> (l k) p", p=P)).then_inc(vecs_loaded, 16)
                sp.dma_start(vec_rows[V_HN:V_HN + 1, :], a["hgrn_out_norm_2"]).then_inc(vecs_loaded, 16)
                sp.dma_start(vec_rows[V_GN:V_GN + 1, :], a["gdn_out_norm_2"]).then_inc(vecs_loaded, 16)
                sp.dma_start(conv_rows, a["gdn_conv_w_2"][0].rearrange("j (n p) -> (j n) p", p=P)).then_inc(vecs_loaded, 16)
                sp.dma_start(ab2[:, 0, :], a["gdn_a_log_2"][0].partition_broadcast(P)).then_inc(vecs_loaded, 16)
                sp.dma_start(ab2[:, 1, :], a["gdn_dt_bias_2"][0].partition_broadcast(P)).then_inc(vecs_loaded, 16)
        c0 = FIRST["ff"]
        load_cols(c0, c0 % RING, w_f1, 0)
        with sp.Fori(0, 5) as i:
            for u in range(3):
                c = c0 + 1 + 2 * u
                load_cols(c + i * 6, c % RING, w_f1, CW * (1 + u) + i * (3 * CW))
                load_rows(c + 1 + i * 6, (c + 1) % RING, w_f2, 2 * u + i * 6)
        c = c0 + 31
        load_rows(c, c % RING, w_f2, 30)
        sp.wait_ge(x_normed, 1)
        for i, name in enumerate(("ln2_g", "ln2_b")):
            sp.dma_start(rows[:, i, :], a[name][0].partition_broadcast(P)).then_inc(rows_loaded, 16)

        def ffn(c0, w_up, w_down):
            for n in range(2):
                load_two(c0 + n, (c0 + n) % RING, w_up, P * n, FF2 + P * n)
            with sp.Fori(0, 5) as i:
                for u in range(2):
                    c = c0 + 2 + 3 * u
                    for n in range(2):
                        tile = 2 + 2 * u + n
                        load_two(c + n + i * 6, (c + n) % RING, w_up, P * tile + i * (4 * P), FF2 + P * tile + i * (4 * P))
                    load_rows(c + 2 + i * 6, (c + 2) % RING, w_down, 2 * u + i * 4)
            load_rows(c0 + 32, (c0 + 32) % RING, w_down, 20)

        ffn(FIRST["ffn1"], w_up1, w_down1)
        c = FIRST["ba"]
        load_cols(c, c % RING, w_in2, O_GA)
        c0 = FIRST["heads"]
        with sp.Fori(0, GH) as h:
            for j, (left, right, step) in enumerate(((O_HQ, O_HF, P), (O_HI, O_HG, P), (O_GQ, O_GK, P),
                                                     (O_GV, O_GV + P, CW), (O_GTH, O_GTG, P), (O_GZ, O_GZ + P, CW))):
                load_two(c0 + j + h * 6, (c0 + j) % RING, w_in2, left + h * step, right + h * step)
        for n in range(4):
            c = FIRST["yh"] + n
            load_cols(c, c % RING, w_bh, CW * n)
        for n in range(8):
            c = FIRST["yg"] + n
            slot_free(c)
            view = w_raw[:, c % RING, :].rearrange("p (k c) -> p k c", c=P)
            for k in (0, 8):
                sp.dma_start(view[:, k:k + 8, :], w_bg[:, k:k + 8, P * n:P * n + P]).then_inc(w_loaded[c % RING], 16)
        for u in range(4):
            c = FIRST["wout2"] + u
            load_rows(c, c % RING, w_out2, 2 * u)
        ffn(FIRST["ffn2"], w_up2, w_down2)
        sp.dma_start(fin_row, a["final_norm_2"].partition_broadcast(P)).then_inc(rows_loaded, 16)
        sp.wait_ge(x_normed, 6)
        o_d = out[0].rearrange("(i p) d -> i p d", p=P)
        for i in range(TT):
            sp.dma_start(o_d[i], tmp[:, i, :]).then_inc(stored, 16)
        sp.wait_ge(stored, 16 * TT)

    @block.gpsimd
    def _(pool):
        b = [0]

        def done(ins):
            b[0] += 1
            ins.then_inc(built, 1)

        def settle():
            pool.wait_ge(built, b[0])

        def low(c, slot):
            pool.wait_ge(hi_ready, c + 1)
            nc.gpsimd.tensor_tensor(w_lo[:, slot, :], w_raw[:, slot, :], w_hi[:, slot, :].bitcast(F32),
                                    ALU.subtract).then_inc(lo_ready, 1)

        def blocks02(ap):
            return ap.rearrange("p (b c) -> p b c", b=3)[:, 0:3:2, :]

        done(nc.gpsimd.memset(ident[:], 0.0))
        done(nc.gpsimd.memset(ones[:], 1.0))
        settle()
        done(nc.gpsimd.affine_select(out=ident[:], in_=ident[:], pattern=[[-1, P]], compare_op=ALU.not_equal,
                                     fill=1.0, base=0, channel_multiplier=1))
        done(nc.gpsimd.memset(tri[:], 1.0))
        done(nc.gpsimd.memset(below[:], 1.0))
        done(nc.gpsimd.memset(caus, 0.0))
        done(nc.gpsimd.memset(strict, 1.0))
        done(nc.gpsimd.memset(eps[:, 0:1], LN_EPS))
        done(nc.gpsimd.memset(eps[:, 1:2], RMS_EPS))
        for h in range(NH):
            done(nc.gpsimd.memset(slopes[:, h:h + 1], -(2.0 ** (-8.0 * (h + 1) / NH))))
        done(nc.gpsimd.memset(lmask[:], 0.0))
        done(nc.gpsimd.memset(lmask_t[:], 0.0))
        settle()
        done(nc.gpsimd.affine_select(out=tri[:], in_=tri[:], pattern=[[1, P]], compare_op=ALU.is_ge,
                                     fill=0.0, base=0, channel_multiplier=-1))
        done(nc.gpsimd.affine_select(out=below[:], in_=below[:], pattern=[[-1, P]], compare_op=ALU.is_gt,
                                     fill=0.0, base=0, channel_multiplier=1))
        done(nc.gpsimd.affine_select(out=blocks02(caus), in_=blocks02(caus), pattern=[[0, 2], [-1, P]],
                                     compare_op=ALU.is_ge, fill=NEG, base=0, channel_multiplier=1))
        done(nc.gpsimd.affine_select(out=blocks02(strict), in_=blocks02(strict), pattern=[[0, 2], [1, P]],
                                     compare_op=ALU.is_gt, fill=0.0, base=0, channel_multiplier=-1))
        done(nc.gpsimd.iota(dist[:, 0:P], pattern=[[-1, P]], base=0, channel_multiplier=1,
                            allow_small_or_imprecise_dtypes=True))
        done(nc.gpsimd.iota(dist[:, P:3 * P], pattern=[[-1, T]], base=P, channel_multiplier=1,
                            allow_small_or_imprecise_dtypes=True))

        def level(l):
            sz = 1 << l
            nb = P // (2 * sz)
            right = lmask[:, l, :].rearrange("p (n h s) -> p n h s", h=2, s=sz)[:, :, 1, :]
            left = lmask_t[:, l, :].rearrange("p (n h s) -> p n h s", h=2, s=sz)[:, :, 0, :]
            for view, base in ((right, 0), (left, -sz)):
                done(nc.gpsimd.memset(view, 1.0))
                settle()
                done(nc.gpsimd.affine_select(out=view, in_=view, pattern=[[-2 * sz, nb], [0, sz]],
                                             compare_op=ALU.is_ge, fill=0.0, base=base, channel_multiplier=1))
                settle()
                done(nc.gpsimd.affine_select(out=view, in_=view, pattern=[[2 * sz, nb], [0, sz]],
                                             compare_op=ALU.is_ge, fill=0.0, base=sz - 1 - base, channel_multiplier=-1))

        static = 10
        for c in range(static):
            low(c, c % RING)
            if 1 <= c <= 7:
                level(c - 1)
        loops = (CHUNKS - static) // RING
        with pool.Fori(0, loops) as i:
            for u in range(RING):
                low(static + u + i * RING, (static + u) % RING)
        for c in range(static + loops * RING, CHUNKS):
            low(c, c % RING)
    BUILT_ID = 3
    BUILT_MASKS = 2 + 1 + 6 + NH + 2 + 6
    BUILT_ALL = BUILT_MASKS + 7 * 6

    @block.scalar
    def _(act):
        def settle():
            nc.scalar.drain()

        def split(base, i=0, step=0):
            slot, c = base % RING, base + i * step
            if isinstance(c, int) and c >= CHUNKS:
                return
            act.wait_ge(w_loaded[slot], 32 * (base // RING + 1) + (32 if slot == 0 else 0) + i * (32 * step // RING))
            if base >= RING:
                act.wait_ge(gemm_done, c - RING + 1)
            nc.scalar.activation(w_hi[:, slot, :], w_raw[:, slot, :], ACT.Copy).then_inc(hi_ready, 1)

        def x_hi(n):
            for h in range(2):
                act.wait_ge(xt_done, n + h + 1)
                nc.scalar.activation(xa_hi[:, 4 * h:4 * h + 4, :].rearrange("p k t -> p (k t)"),
                                     M[:, 2 * h:2 * h + 2, :].rearrange("p b c -> p (b c)"), ACT.Copy).then_inc(xh_ready, 1)

        x_hi(0)
        for c in range(RING + 1):
            split(c)
        act.wait_ge(fg_ready, 1)
        nc.scalar.activation(fgn, fgx, ACT.Abs)
        settle()
        nc.scalar.activation(fgn, fgn, ACT.Exp, scale=-1.0)
        settle()
        nc.scalar.activation(fgn, fgn, ACT.Ln, bias=1.0).then_inc(fln_ready, 1)

        def relu_dots(u):
            act.wait_ge(dots_done, u + 1)
            if u >= 1:
                act.wait_ge(relu_used, u)
            nc.scalar.activation(relu_d, M[:, 0:4, 0:3 * P], ACT.Relu).then_inc(relu_ready, 1)

        def gate_exp(c, bank, tile):
            act.wait_ge(gemm_done, c + 1)
            nc.scalar.activation(gates[:, ds(tile, 2), :].rearrange("p n t -> p (n t)"), G[:, bank, :],
                                 ACT.Exp, scale=-1.0).then_inc(evac[bank], 1)

        for c in range(FIRST["qi"], FIRST["pairs"]):
            split(c + RING)
            if c in (2, 3, 4, 5):
                relu_dots(c - 2)
            if c >= FIRST["gates"]:
                gate_exp(c, c % 2, 2 * (c - FIRST["gates"]))

        c0 = FIRST["pairs"]

        def softmax_exp(n, lg, p):
            act.wait_ge(max_ready[n], p + 1)
            for e in range(2):
                for i, (lo_, hi_) in enumerate(((0, P), (P, 3 * P))):
                    ins = nc.scalar.activation(lg[:, e, lo_:hi_], lg[:, e, lo_:hi_], ACT.Exp,
                                               bias=nmx[n][:, i, e:e + 1], accum_out=rsum[n][:, i, e:e + 1])
            ins.then_inc(exp_ready[n], 1)

        def pt_copy(n, bank, dst, p):
            act.wait_ge(pt_done[n], p + 1)
            nc.scalar.activation(dst, M[:, bank:bank + 2, 0:3 * P], ACT.Copy).then_inc(pt_ready[n], 1)

        def o_hi(n, bank, p):
            act.wait_ge(o_done[n], p + 1)
            nc.scalar.activation(xb_hi[:, ds(4 * n + p, 1), :].rearrange("p k t -> p (k t)"),
                                 M[:, bank, 0:T], ACT.Copy).then_inc(oh_ready[n], 1)

        with act.Fori(0, PAIRS) as p:
            split(c0 + 0 + RING, p, 6)
            split(c0 + 1 + RING, p, 6)
            act.wait_ge(z_done, p + 1)
            nc.scalar.activation(st1, M[:, 4:6, 0:3 * P], ACT.Abs)
            settle()
            nc.scalar.activation(st1, st1, ACT.Exp, scale=-1.0)
            settle()
            nc.scalar.activation(st1, st1, ACT.Ln, bias=1.0).then_inc(sp_ready, 1)
            split(c0 + 2 + RING, p, 6)
            softmax_exp(0, log_a, p)
            split(c0 + 3 + RING, p, 6)
            act.wait_ge(lb_ready, p + 1)
            nc.scalar.activation(st2, st2, ACT.Exp).then_inc(ex_ready, 1)
            softmax_exp(1, log_fo, p)
            pt_copy(0, 0, pt_a, p)
            split(c0 + 4 + RING, p, 6)
            gate_exp(c0 + 4 + p * 6, (c0 + 4) % 2, 8 + p * 4)
            o_hi(2, 4, p)
            o_hi(0, 0, p)
            pt_copy(1, 2, pt_f, p)
            split(c0 + 5 + RING, p, 6)
            gate_exp(c0 + 5 + p * 6, (c0 + 5) % 2, 10 + p * 4)
            o_hi(1, 2, p)

        c0 = FIRST["branch"]
        with act.Fori(0, 2) as half:
            for i in range(3):
                split(c0 + i + RING, half, 3)
            act.wait_ge(mrg_ready, half + 1)
            nc.scalar.activation(xa_hi[:, ds(half * 4, 4), :].rearrange("p k t -> p (k t)"), mrg,
                                 ACT.Copy).then_inc(mh_ready, 1)
        c0 = FIRST["wout"]
        for c in range(c0, c0 + 4):
            split(c + RING)

        def rstd(n):
            act.wait_ge(var_ready, n)
            nc.scalar.activation(stat[:, 32:34], stat[:, 30:32], ACT.Ln, bias=eps[:, 0:1])
            settle()
            nc.scalar.activation(stat[:, 34:36], stat[:, 32:34], ACT.Exp, scale=-0.5).then_inc(rstd_ready, 1)

        act.wait_ge(built, BUILT_MASKS)
        rstd(1)
        x_hi(2)

        def ff_relu(c, r):
            act.wait_ge(gemm_done, c + 1)
            nc.scalar.activation(ffr[:, r, :], ffbank(r), ACT.Relu).then_inc(ffr_ready, 1)

        def ff_hi(r, turn):
            act.wait_ge(evac[r], EV_FF[r] + turn + 1)
            nc.scalar.activation(xb_hi[:, 2 * r:2 * r + 2, :].rearrange("p k t -> p (k t)"), ffs[:, r, :],
                                 ACT.Copy).then_inc(hh_ready, 1)

        c0 = FIRST["ff"]
        split(c0 + RING)
        ff_relu(c0, 0)
        ff_hi(0, 0)
        with act.Fori(0, 5) as i:
            for u in range(3):
                c = c0 + 1 + 2 * u
                r = (1 + u) % 3
                split(c + RING, i, 6)
                ff_relu(c + i * 6, r)
                ff_hi(r, (1 + u) // 3 + i)
                split(c + 1 + RING, i, 6)
        split(c0 + 31 + RING)
        rstd(2)
        def rms_rstd(n, semaphore, count):
            act.wait_ge(semaphore, count)
            for i in range(TT):
                nc.scalar.activation(tmp[:, i, :], res[:, i, :], ACT.Square, accum_out=stat[:, 40 + i:41 + i])
            settle()
            nc.scalar.activation(stat[:, 42:44], stat[:, 40:42], ACT.Ln, scale=1.0 / D, bias=eps[:, 1:2])
            settle()
            nc.scalar.activation(stat[:, 44:46], stat[:, 42:44], ACT.Exp, scale=-0.5).then_inc(rstd_ready, 1)

        def gain_hi(n, gain):
            for k in range(KT):
                if k % 4 == 0:
                    act.wait_ge(xt_done, n + k // 4 + 1)
                ins = nc.scalar.activation(xa_hi[:, k, :], M[:, k // 2, T * (k % 2):T * (k % 2) + T], ACT.Copy,
                                           scale=vec[:, gain + k:gain + k + 1])
                if k % 4 == 3:
                    ins.then_inc(xh_ready, 1)

        def ffn(c0, ev):
            def hidden(c, i, step, n, turn, tile):
                split(c + RING, i, step)
                act.wait_ge(gemm_done, c + 1 + i * step)
                nc.scalar.activation(ffn_s[:, n, :], G[:, n, 0:T], ACT.Silu).then_inc(ffr_ready, 1)
                act.wait_ge(evac[n], ev[n] + turn + 1)
                nc.scalar.activation(xb_hi[:, tile, :], ffn_h[:, n, :], ACT.Copy).then_inc(hh_ready, 1)

            def steps(i):
                for u in range(2):
                    c = c0 + 2 + 3 * u
                    for n in range(2):
                        hidden(c + n, i, 6, n, 1 + u + i * 2, (1 + u) % 2 * 2 + n)
                    split(c + 2 + RING, i, 6)

            for n in range(2):
                hidden(c0 + n, 0, 0, n, 0, n)
            with act.Fori(0, 4) as i:
                steps(i)
            steps(4)
            split(c0 + 32 + RING)

        act.wait_ge(vec_ready, 1)
        rms_rstd(3, x_normed, 2)
        gain_hi(4, V_FFN1)
        ffn(FIRST["ffn1"], EV_FFN1)
        rms_rstd(4, y_used, 3)
        gain_hi(6, V_MIX)
        nc.scalar.activation(lb, lb, ACT.Exp)
        nc.scalar.activation(lb1, lb1, ACT.Exp).then_inc(lb_exp, 1)
        c = FIRST["ba"]
        split(c + RING)
        act.wait_ge(ab_ready, 1)
        nc.scalar.activation(abn, abx[:, :, 0:VH], ACT.Abs)
        nc.scalar.activation(ab2[:, 0, :], ab2[:, 0, :], ACT.Exp)
        nc.scalar.activation(beta, abx[:, :, VH:2 * VH], ACT.Exp, scale=-1.0)
        settle()
        nc.scalar.activation(abn, abn, ACT.Exp, scale=-1.0)
        settle()
        nc.scalar.activation(abn, abn, ACT.Ln, bias=1.0).then_inc(abln_ready, 1)

        c0 = FIRST["heads"]

        def head(i, gemm, main, tail, step):
            base = 0 if step else 6 * i if isinstance(i, int) else 0
            k, st = (i, 6) if step else (0, 0)

            def split_j(j):
                if gemm:
                    split(c0 + j + RING + base, k, st)

            def chunk_done(j):
                act.wait_ge(gemm_done, c0 + j + 1 + i * 6)

            def level_exp(l):
                if not gemm:
                    return
                act.wait_ge(dd_ready, l + i * 8)
                buf = dd[:, l % 2, :]
                if l == 8:
                    nc.scalar.activation(buf[:, 0:P], buf[:, 0:P], ACT.Exp, scale=-1.0)
                    nc.scalar.activation(buf[:, P:T], hb[:, P:T], ACT.Exp).then_inc(lev_exp, 1)
                    return
                half = buf.rearrange("p (n h s) -> p n h s", h=2, s=1 << (l - 1))
                nc.scalar.activation(half[:, :, 0, :], half[:, :, 0, :], ACT.Exp, scale=-1.0)
                nc.scalar.activation(half[:, :, 1, :], half[:, :, 1, :], ACT.Exp).then_inc(lev_exp, 1)

            def inv_copy(dst, t):
                act.wait_ge(t_done, t + 1 + (i - 1) * 7)
                nc.scalar.activation(dst, M[:, 5, :].rearrange("p (i e c) -> p i e c", i=TT, e=2), ACT.Copy).then_inc(t_ready, 1)

            def z_copy(l):
                act.wait_ge(zz_done, l + (i - 1) * 6)
                nc.scalar.activation(zi, M[:, 3, :].rearrange("p (i e c) -> p i e c", i=TT, e=2), ACT.Copy).then_inc(zc_ready, 1)

            hprev = not isinstance(i, int) or 1 <= i <= GH
            if hprev:
                act.wait_ge(hpv_done, i)
                nc.scalar.activation(hsq, M[:, 1, 0:T], ACT.Square).then_inc(hsq_ready, 1)
                act.wait_ge(hss_done, i)
                nc.scalar.activation(hrs, M[:, 1, T:2 * T], ACT.Ln, scale=1.0 / P, bias=eps[:, 1:2])
                settle()
                nc.scalar.activation(hrs, hrs, ACT.Exp, scale=-0.5).then_inc(hrs_ready, 1)
            if gemm:
                chunk_done(0)
                nc.scalar.activation(eh, G[:, 1, :], ACT.Exp, scale=-1.0).then_inc(eh_ready, 1)
                split_j(0)
            if main:
                act.wait_ge(conv_ready, i)
                nc.scalar.activation(eg, acc.rearrange("p n t -> p (n t)"), ACT.Exp, scale=-1.0).then_inc(ec_ready, 1)
            if gemm:
                act.wait_ge(f_ready, i + 1)
                nc.scalar.activation(hf, hf, ACT.Ln).then_inc(lnf_ready, 1)
            if tail:
                act.wait_ge(go_done, i - 1)
                nc.scalar.activation(zi, M[:, 5, :].rearrange("p (i e c) -> p i e c", i=TT, e=2), ACT.Square).then_inc(gsq_ready, 1)
            if gemm:
                after(act, hfin, i)
                chunk_done(1)
                nc.scalar.activation(hsg, G[:, 0, T:2 * T], ACT.Exp, scale=-1.0).then_inc(hgx_ready, 1)
                split_j(1)
            if tail:
                act.wait_ge(gss_done, i - 1)
                nc.scalar.activation(xi, M[:, 2, :].rearrange("p (i e c) -> p i e c", i=TT, e=2), ACT.Ln, scale=1.0 / P,
                                     bias=eps[:, 1:2])
                settle()
                nc.scalar.activation(xi, xi, ACT.Exp, scale=-0.5).then_inc(grs_ready, 1)
                act.wait_ge(og_ready, i - 1)
                nc.scalar.activation(xb_hi[:, ds(i * 2 - 4, 2), :].rearrange("p k t -> p (k t)"),
                                     zi.rearrange("p i e c -> p (i e c)"), ACT.Copy).then_inc(ogh_ready, 1)
            if main:
                act.wait_ge(act_ready, i)
                nc.scalar.activation(eg[:, 0:2 * T], acc[:, 0:2, :].rearrange("p n t -> p (n t)"), ACT.Square).then_inc(sq_ready, 1)
                act.wait_ge(ss_done, i)
                nc.scalar.activation(eg[:, 2 * T:4 * T], M[:, 5, :], ACT.Ln, bias=eps[:, 1:2])
                settle()
                nc.scalar.activation(eg[:, 2 * T:4 * T], eg[:, 2 * T:4 * T], ACT.Exp, scale=-0.5).then_inc(rs_ready, 1)
                act.wait_ge(vt_done, i)
                nc.scalar.activation(vsd, M[:, 4, :].rearrange("p (i e c) -> p i e c", i=TT, e=2), ACT.Copy).then_inc(v_ready, 1)
            level_exp(1)
            if main:
                act.wait_ge(lt_pre, i)
                nc.scalar.activation(lt, lt, ACT.Exp).then_inc(lt_ready, 1)
            level_exp(2)
            level_exp(3)
            if main:
                inv_copy(xi, 0)
            split_j(2)
            if main:
                z_copy(1)
            level_exp(4)
            if main:
                inv_copy(yi, 1)
                z_copy(2)
            level_exp(5)
            split_j(3)
            if main:
                inv_copy(yi, 2)
                z_copy(3)
            level_exp(6)
            if main:
                inv_copy(yi, 3)
                z_copy(4)
            level_exp(7)
            split_j(4)
            if gemm:
                chunk_done(4)
                nc.scalar.activation(gates2[:, ds(i, 1), :, :].rearrange("p n b t -> p (n b t)"), G[:, 1, :], ACT.Exp,
                                     scale=-1.0).then_inc(evac[1], 1)
            if main:
                inv_copy(yi, 4)
                z_copy(5)
            level_exp(8)
            if main:
                inv_copy(yi, 5)
                z_copy(6)
            split_j(5)
            if gemm:
                chunk_done(5)
                if main:
                    act.wait_ge(sgz_moved, i)
                nc.scalar.activation(sgz, G[:, 0, :].rearrange("p (e t) -> p e t", e=2), ACT.Exp, scale=-1.0).then_inc(gzx_ready, 1)
            if main:
                inv_copy(yi, 6)

        head(0, True, False, False, 0)
        head(1, True, True, False, 0)
        with act.Fori(2, GH) as i:
            head(i, True, True, True, 6)
        head(GH, False, True, True, 0)
        head(GH + 1, False, False, True, 0)

        for h in range(2):
            act.wait_ge(hfin, GH)
            nc.scalar.activation(xa_hi[:, 4 * h:4 * h + 4, :].rearrange("p k t -> p (k t)"),
                                 o_h[:, 4 * h:4 * h + 4, :].rearrange("p k t -> p (k t)"), ACT.Copy).then_inc(ohh_ready, 1)
        for c in range(FIRST["yh"], FIRST["wout2"]):
            split(c + RING)
        for h in range(2):
            act.wait_ge(ym_ready, 4 * h + 4)
            nc.scalar.activation(xa_hi[:, 4 * h:4 * h + 4, :].rearrange("p k t -> p (k t)"),
                                 o_h[:, 4 * h:4 * h + 4, :].rearrange("p k t -> p (k t)"), ACT.Copy).then_inc(ymh_ready, 1)
        for c in range(FIRST["wout2"], FIRST["ffn2"]):
            split(c + RING)
        rms_rstd(5, y_used, 4)
        gain_hi(8, V_FFN2)
        ffn(FIRST["ffn2"], EV_FFN2)
        rms_rstd(6, y_used, 5)

    @block.vector
    def _(dve):
        v = nc.vector

        def settle():
            v.drain()

        def low_of(dst, src, hi):
            return v.tensor_tensor(dst, src, hi.bitcast(F32), ALU.subtract)

        def x_low(n):
            for h in range(2):
                dve.wait_ge(xh_ready, n + h + 1)
                low_of(xa_lo[:, 4 * h:4 * h + 4, :].rearrange("p k t -> p (k t)"),
                       M[:, 2 * h:2 * h + 2, :].rearrange("p b c -> p (b c)"),
                       xa_hi[:, 4 * h:4 * h + 4, :].rearrange("p k t -> p (k t)")).then_inc(xl_ready, 1)

        x_low(0)
        dve.wait_ge(gemm_done, 1)
        v.tensor_copy(ki_t, G[:, 0, 0:T])
        v.tensor_copy(wi[:, :, :], G[:, 0, T:T + 48].rearrange("p (i h) -> p i h", i=TT)).then_inc(evac[0], 1)
        settle()
        dve.wait_ge(par_loaded, 16)
        v.tensor_tensor(fgx, wi[:, :, IDXH:24], bfor.unsqueeze(1).to_broadcast([P, TT, NH]), ALU.add)
        settle()
        v.tensor_scalar(log_f, fgx, 0.0, None, ALU.min).then_inc(fg_ready, 1)

        def qi_copy(u):
            c = FIRST["qi"] + u
            dve.wait_ge(gemm_done, c + 1)
            if u >= 2:
                dve.wait_ge(dots_done, u - 1)
            v.tensor_copy(qi_t[:, u % 2, :], G[:, c % 2, :]).then_inc(evac[c % 2], 1)

        def add_scores(u):
            dve.wait_ge(relu_ready, u + 1)
            for e in range(4):
                h = 4 * u + e
                for i, (lo_, hi_) in enumerate(((0, P), (P, 3 * P))):
                    if h == 0:
                        ins = v.tensor_scalar(score[:, lo_:hi_], relu_d[:, e, lo_:hi_], wi[:, i, h:h + 1], None, ALU.mult)
                    else:
                        ins = v.scalar_tensor_tensor(out=score[:, lo_:hi_], in0=relu_d[:, e, lo_:hi_],
                                                     scalar=wi[:, i, h:h + 1], in1=score[:, lo_:hi_],
                                                     op0=ALU.mult, op1=ALU.add)
                if e == 3:
                    ins.then_inc(relu_used, 1)
                settle()

        def va_copy(u):
            c = FIRST["va"] + u
            dve.wait_ge(gemm_done, c + 1)
            v.tensor_copy(va[:, :, CW * u:CW * u + CW], G[:, c % 2, :].rearrange("p (i c) -> p i c", i=TT)
                          ).then_inc(evac[c % 2], 1)

        qi_copy(0)
        dve.wait_ge(fln_ready, 1)
        v.tensor_tensor(log_f, log_f, fgn, ALU.subtract).then_inc(logf_ready, 1)
        qi_copy(1)
        add_scores(0)
        dve.wait_ge(cum_done, 1)
        v.tensor_copy(c_f, M[:, 5, 0:TT * NH].rearrange("p (i h) -> p i h", i=TT)).then_inc(c_ready, 1)
        qi_copy(2)
        add_scores(1)
        qi_copy(3)
        add_scores(2)
        va_copy(0)
        add_scores(3)
        va_copy(1)
        dve.wait_ge(built, BUILT_MASKS)
        v.tensor_tensor(score, score, caus, ALU.add)
        settle()
        tiles = ((0, P), (P, 3 * P))
        for _ in range(TOPK // 8):
            for i, (lo_, hi_) in enumerate(tiles):
                v.max(out=top8[:, i, :], in_=score[:, lo_:hi_])
            settle()
            for i, (lo_, hi_) in enumerate(tiles):
                v.match_replace(out=score[:, lo_:hi_], in_to_replace=top8[:, i, :], in_values=score[:, lo_:hi_],
                                imm_value=TAKEN)
            settle()
        v.tensor_scalar(selb, score, TAKEN / 2, NEG, ALU.is_gt, ALU.mult)
        settle()
        v.tensor_tensor(selb, selb, caus, ALU.add)
        settle()

        c0 = FIRST["pairs"]

        def sigmoid(tile, n):
            sl = gates[:, ds(tile, n), :].rearrange("p n t -> p (n t)")
            v.tensor_scalar(sl, sl, 1.0, None, ALU.add)
            settle()
            v.reciprocal(sl, sl)

        dve.wait_ge(evac[0], c0 // 2 + 1)
        dve.wait_ge(evac[1], c0 // 2)
        sigmoid(0, 8)

        def pair_copy(j, p, q_t, k_t, read):
            dve.wait_ge(gemm_done, c0 + j + 1 + p * 6)
            bank = (c0 + j) % 2
            v.tensor_scalar(q_t, G[:, bank, 0:T], HD ** -0.5, None, ALU.mult)
            v.tensor_copy(k_t, G[:, bank, T:2 * T]).then_inc(evac[bank], 1)

        def row_max(n, lg):
            settle()
            v.tensor_reduce(nmx[n][:, 0, :], lg[:, :, 0:P], AX_X, ALU.max, negate=True)
            v.tensor_reduce(nmx[n][:, 1, :], lg[:, :, P:3 * P], AX_X, ALU.max, negate=True).then_inc(max_ready[n], 1)

        def normalise(n, lg, p):
            dve.wait_ge(exp_ready[n], p + 1)
            v.reciprocal(rinv[n], rsum[n])
            settle()
            for e in range(2):
                for i, (lo_, hi_) in enumerate(tiles):
                    ins = v.tensor_scalar(lg[:, e, lo_:hi_], lg[:, e, lo_:hi_], rinv[n][:, i, e:e + 1], None, ALU.mult)
            ins.then_inc(prob_ready[n], 1)

        def o_low(n, bank, p):
            dve.wait_ge(oh_ready[n], p + 1)
            low_of(xb_lo[:, ds(4 * n + p, 1), :].rearrange("p k t -> p (k t)"), M[:, bank, 0:T],
                   xb_hi[:, ds(4 * n + p, 1), :].rearrange("p k t -> p (k t)")).then_inc(ol_ready[n], 1)

        def both(ap):
            return ap.unsqueeze(1).to_broadcast([P, 2, ap.shape[-1]])

        with dve.Fori(0, PAIRS) as p:
            v.tensor_copy(fbc, log_f[:, :, ds(p * 2, 2)].unsqueeze(3).to_broadcast([P, TT, 2, P])).then_inc(fbc_ready, 1)
            v.tensor_copy(cq, c_f[:, :, ds(p * 2, 2)])
            v.tensor_copy(va_p, va[:, :, ds(p * P, P)]).then_inc(va_ready, 1)
            pair_copy(0, p, qs_t, ks_t, None)
            for e in range(2):
                v.scalar_tensor_tensor(out=log_a[:, e, :], in0=dist, scalar=slopes[:, ds(p * 2 + e, 1)], in1=selb,
                                       op0=ALU.mult, op1=ALU.add)
            pair_copy(1, p, qa_t, ka_t, None)
            dve.wait_ge(sp_ready, p + 1)
            z = M[:, 4:6, 0:3 * P]
            v.scalar_tensor_tensor(out=st1, in0=z, scalar=0.0, in1=st1, op0=ALU.max, op1=ALU.add)
            settle()
            v.tensor_tensor(st2, z, st1, ALU.subtract)
            v.scalar_tensor_tensor(out=st3, in0=st1, scalar=-1.0, in1=both(strict), op0=ALU.mult, op1=ALU.mult
                                   ).then_inc(lom_ready, 1)
            dve.wait_ge(ck_done, p + 1)
            v.tensor_tensor(log_fo[:, :, 0:P], both(caus[:, 0:P]), M[:, 2:4, 0:P], ALU.subtract)
            v.tensor_tensor(log_fo[:, :, P:3 * P], both(caus[:, P:3 * P]), M[:, 2:4, 0:T], ALU.subtract
                            ).then_inc(mck_ready, 1)
            pair_copy(2, p, qf_t, kf_t, None)
            dve.wait_ge(sc_done[0], p + 1)
            v.tensor_tensor(log_a, M[:, 0:2, 0:3 * P], log_a, ALU.add)
            row_max(0, log_a)
            dve.wait_ge(gemm_done, c0 + 4 + p * 6)
            v.tensor_copy(vfs, G[:, (c0 + 3) % 2, :].rearrange("p (i c) -> p i c", i=TT)).then_inc(evac[(c0 + 3) % 2], 1)
            normalise(0, log_a, p)
            dve.wait_ge(later_done, p + 1)
            v.tensor_tensor(st2, M[:, 4:6, 0:3 * P], st2, ALU.add).then_inc(lb_ready, 1)
            dve.wait_ge(sc_done[1], p + 1)
            for e in range(2):
                for i, (lo_, hi_) in enumerate(tiles):
                    v.scalar_tensor_tensor(out=log_fo[:, e, lo_:hi_], in0=M[:, 2 + e, lo_:hi_], scalar=cq[:, i, e:e + 1],
                                           in1=log_fo[:, e, lo_:hi_], op0=ALU.add, op1=ALU.add)
            row_max(1, log_fo)
            dve.wait_ge(ex_ready, p + 1)
            v.tensor_tensor(st2, st2, both(strict), ALU.mult).then_inc(stick_ready, 1)
            normalise(1, log_fo, p)
            o_low(2, 4, p)
            o_low(0, 0, p)
            for j in (4, 5):
                dve.wait_ge(evac[(c0 + j) % 2], (c0 + j) // 2 + 1 + p * 3)
            sigmoid(8 + p * 4, 4)
            o_low(1, 2, p)
        settle()

        c0 = FIRST["branch"]
        with dve.Fori(0, 2) as half:
            for i in range(3):
                dve.wait_ge(gemm_done, c0 + i + 1 + half * 3)
                up = M[:, 2 * i:2 * i + 2, :].rearrange("p b c -> p (b c)")
                sg = gates[:, ds(8 * i + half * 4, 4), :].rearrange("p n t -> p (n t)")
                if i == 0:
                    v.tensor_tensor(mrg, up, sg, ALU.mult).then_inc(branch_used, 1)
                else:
                    v.tensor_tensor(mrg2, up, sg, ALU.mult).then_inc(branch_used, 1)
                    settle()
                    ins = v.tensor_tensor(mrg, mrg, mrg2, ALU.add)
                    if i == 2:
                        ins.then_inc(mrg_ready, 1)
                    settle()
            dve.wait_ge(mh_ready, half + 1)
            low_of(xa_lo[:, ds(half * 4, 4), :].rearrange("p k t -> p (k t)"), mrg,
                   xa_hi[:, ds(half * 4, 4), :].rearrange("p k t -> p (k t)")).then_inc(ml_ready, 1)
            settle()

        def residual(scale_x, scale_y):
            for i in range(TT):
                y = M[:, 2 * i:2 * i + 2, :].rearrange("p b c -> p (b c)")
                if scale_y == 1.0:
                    ins = v.scalar_tensor_tensor(out=res[:, i, :], in0=res[:, i, :], scalar=scale_x, in1=y,
                                                 op0=ALU.mult, op1=ALU.add)
                else:
                    ins = v.scalar_tensor_tensor(out=res[:, i, :], in0=y, scalar=scale_y, in1=res[:, i, :],
                                                 op0=ALU.mult, op1=ALU.add)
            ins.then_inc(y_used, 1)
            settle()

        def layer_norm(n):
            bn = stat[:, 0:24].rearrange("p (i h s) -> p i h s", i=TT, h=2)
            mv = stat[:, 24:28].rearrange("p (i s) -> p i s", i=TT)
            for i in range(TT):
                for h in range(2):
                    v.bn_stats(out=bn[:, i, h, :], in_=res[:, i, 512 * h:512 * h + 512])
            settle()
            for i in range(TT):
                v.bn_aggr(out=mv[:, i, :], in_=bn[:, i, :, :])
            settle()
            v.tensor_copy(stat[:, 30:32], mv[:, :, 1]).then_inc(var_ready, 1)
            dve.wait_ge(rstd_ready, n)
            for i in range(TT):
                v.tensor_scalar(tmp[:, i, :], res[:, i, :], mv[:, i, 0:1], stat[:, 34 + i:35 + i], ALU.subtract, ALU.mult)
            settle()
            dve.wait_ge(rows_loaded, 32 * n)
            v.tensor_tensor(tmp, tmp, rows[:, 0, :].unsqueeze(1).to_broadcast([P, TT, D]), ALU.mult)
            settle()
            v.tensor_tensor(res[:], tmp, rows[:, 1, :].unsqueeze(1).to_broadcast([P, TT, D]), ALU.add).then_inc(x_normed, 1)
            settle()

        dve.wait_ge(gemm_done, FIRST["ff"])
        residual(ALPHA, 1.0)
        layer_norm(1)
        x_low(2)
        dve.wait_ge(vec_done, 1)
        v.tensor_copy(vec[:, 0:VECS], M[:, 4, 0:VECS])
        v.tensor_copy(conv.rearrange("p j n -> p (j n)"), M[:, 4, P:2 * P])
        settle()
        v.tensor_tensor(lb, vec[:, V_LB1:V_LB1 + GH], vec[:, V_LB0:V_LB0 + GH], ALU.subtract)
        v.tensor_tensor(lb1, vec[:, V_LB0:V_LB0 + GH], vec[:, V_LB1:V_LB1 + GH], ALU.subtract).then_inc(vec_ready, 1)

        def ff_square(r, g):
            dve.wait_ge(ffr_ready, g + 1)
            v.scalar_tensor_tensor(out=ffs[:, r, :], in0=ffbank(r), scalar=0.0, in1=ffr[:, r, :],
                                   op0=ALU.max, op1=ALU.mult).then_inc(evac[r], 1)
            dve.wait_ge(hh_ready, g + 1)
            low_of(xb_lo[:, 2 * r:2 * r + 2, :].rearrange("p k t -> p (k t)"), ffs[:, r, :],
                   xb_hi[:, 2 * r:2 * r + 2, :].rearrange("p k t -> p (k t)")).then_inc(h_ready, 1)

        ff_square(0, 0)
        with dve.Fori(0, 5) as i:
            for u in range(3):
                ff_square((1 + u) % 3, 1 + u + i * 3)
        dve.wait_ge(gemm_done, FIRST["ffn1"])
        residual(ALPHA, 1.0)
        layer_norm(2)
        def rms_apply(n):
            dve.wait_ge(rstd_ready, n)
            for i in range(TT):
                ins = v.tensor_scalar(tmp[:, i, :], res[:, i, :], stat[:, 44 + i:45 + i], None, ALU.mult)
            ins.then_inc(x_normed, 1)

        def gain_low(n, gain):
            for k in range(KT):
                if k % 4 == 0:
                    dve.wait_ge(xh_ready, n + k // 4 + 1)
                ins = v.scalar_tensor_tensor(out=xa_lo[:, k, :], in0=M[:, k // 2, T * (k % 2):T * (k % 2) + T],
                                             scalar=vec[:, gain + k:gain + k + 1], in1=xa_hi[:, k, :].bitcast(F32),
                                             op0=ALU.mult, op1=ALU.subtract)
                if k % 4 == 3:
                    ins.then_inc(xl_ready, 1)

        def ffn(c0, h0):
            def hidden(n, tile, k):
                dve.wait_ge(ffr_ready, k + 1)
                v.tensor_tensor(ffn_h[:, n, :], ffn_s[:, n, :], G[:, n, T:2 * T], ALU.mult).then_inc(evac[n], 1)
                dve.wait_ge(hh_ready, k + 1)
                low_of(xb_lo[:, tile, :], ffn_h[:, n, :], xb_hi[:, tile, :]).then_inc(h_ready, 1)

            for n in range(2):
                hidden(n, n, h0 + n)
            with dve.Fori(0, 5) as i:
                for u in range(2):
                    for n in range(2):
                        hidden(n, (1 + u) % 2 * 2 + n, h0 + 2 + 2 * u + n + i * 4)
            dve.wait_ge(gemm_done, c0 + 33)
            residual(1.0, 0.5)

        rms_apply(3)
        gain_low(4, V_FFN1)
        ffn(FIRST["ffn1"], H_FFN1)
        rms_apply(4)
        gain_low(6, V_MIX)

        def plus_one_inverse(ap):
            v.tensor_scalar(ap, ap, 1.0, None, ALU.add)
            settle()
            v.reciprocal(ap, ap)
            settle()

        dve.wait_ge(lb_exp, 1)
        plus_one_inverse(lb)
        plus_one_inverse(lb1)
        v.memset(raw[:, :, 0:4], 0.0)
        dve.wait_ge(gemm_done, FIRST["ba"] + 1)
        v.tensor_copy(abx, G[:, 0, 0:4 * VH].rearrange("p (i h) -> p i h", i=TT)).then_inc(evac[0], 1)
        settle()
        v.tensor_tensor(abx[:, :, 0:VH], abx[:, :, 0:VH], ab2[:, 1, :].unsqueeze(1).to_broadcast([P, TT, VH]), ALU.add)
        v.drain().then_inc(ab_ready, 1)
        dve.wait_ge(abln_ready, 1)
        v.scalar_tensor_tensor(out=gdec, in0=abx[:, :, 0:VH], scalar=0.0, in1=abn, op0=ALU.max, op1=ALU.add)
        plus_one_inverse(beta)
        v.scalar_tensor_tensor(out=gdec, in0=gdec, scalar=-1.0, in1=ab2[:, 0, :].unsqueeze(1).to_broadcast([P, TT, VH]),
                               op0=ALU.mult, op1=ALU.mult).then_inc(g_ready, 1)
        v.tensor_scalar(nbeta, beta, -1.0, None, ALU.mult)
        dve.wait_ge(gsum_done, 1)
        v.tensor_copy(gam, M[:, 4, 0:2 * VH].rearrange("p (i h) -> p i h", i=TT))
        settle()
        v.tensor_tensor(gmx, gam[:, 0, :], M[:, 4, 2 * VH:3 * VH], ALU.subtract)
        settle()

        c0 = FIRST["heads"]

        def m4(b):
            return M[:, b, :].rearrange("p (i e c) -> p i e c", i=TT, e=2)

        def head(i, gemm, main, tail):
            hprev = not isinstance(i, int) or 1 <= i <= GH

            def tap(j):
                if not main:
                    return
                for n in range(4):
                    x = raw[:, n, 1 + j:1 + j + T]
                    w = cwt[:, j, n:n + 1]
                    if j == 0:
                        ins = v.tensor_scalar(acc[:, n, :], x, w, None, ALU.mult)
                    else:
                        ins = v.scalar_tensor_tensor(out=acc[:, n, :], in0=x, scalar=w, in1=acc[:, n, :],
                                                     op0=ALU.mult, op1=ALU.add)
                if j == CONV - 1:
                    ins.then_inc(conv_ready, 1)
                settle()

            def middle(l):
                if not gemm:
                    return
                if l == 8:
                    v.tensor_tensor(dd[:, 0, 0:P], hb[:, 0:P], hb[:, P - 1:P].to_broadcast([P, P]), ALU.subtract
                                    ).then_inc(dd_ready, 1)
                    return
                sz = 1 << (l - 1)
                blocks = hb.rearrange("p (n s) -> p n s", s=2 * sz)
                v.tensor_tensor(dd[:, l % 2, :].rearrange("p (n s) -> p n s", s=2 * sz), blocks,
                                blocks[:, :, sz - 1:sz].to_broadcast([P, P // sz, 2 * sz]), ALU.subtract).then_inc(dd_ready, 1)

            def decayed(l):
                if not gemm:
                    return
                dve.wait_ge(lev_exp, l + i * 8)
                sz = 1 << (l - 1)
                view = [ap.rearrange("p (n h s) -> p n h s", h=2, s=sz) for ap in (kqd[:, l % 2, :], hk, hq, dd[:, l % 2, :])]
                v.tensor_tensor(view[0][:, :, 0, :], view[1][:, :, 0, :], view[3][:, :, 0, :], ALU.mult)
                v.tensor_tensor(view[0][:, :, 1, :], view[2][:, :, 1, :], view[3][:, :, 1, :], ALU.mult).then_inc(wl_ready, 1)

            def scored(l):
                if not gemm:
                    return
                dve.wait_ge(lev_done, l + 1 + i * 9)
                ps = M[:, 0, T * (l % 2):T * (l % 2) + T]
                both_b = [P, 2, P]
                if l == 0:
                    v.tensor_tensor(sct[:, 0:T].rearrange("p (i c) -> p i c", i=2), ps.rearrange("p (i c) -> p i c", i=2),
                                    ident[:].unsqueeze(1).to_broadcast(both_b), ALU.mult).then_inc(sc_used, 1)
                elif l == 8:
                    v.tensor_copy(sct[:, T:3 * P], ps[:, 0:P]).then_inc(sc_used, 1)
                else:
                    dve.sem_inc(waited, 1)
                    v.copy_predicated(sct[:, 0:T].rearrange("p (i c) -> p i c", i=2),
                                      lmask[:, l - 1, :].bitcast(I32).unsqueeze(1).to_broadcast(both_b),
                                      ps.rearrange("p (i c) -> p i c", i=2)).then_inc(sc_used, 1)
                settle()

            def inverse(l):
                if not main:
                    return
                dve.wait_ge(ww_done, l + (i - 1) * 6)
                dve.sem_inc(waited, 1)
                v.copy_predicated(xi, lmask_t[:, l, :].bitcast(I32).unsqueeze(1).unsqueeze(1).to_broadcast([P, TT, 2, P]),
                                  m4(4)).then_inc(xx_ready, 1)

            def chunk_done(j):
                dve.wait_ge(gemm_done, c0 + j + 1 + i * 6)

            if main:
                h = i - 1
                v.tensor_copy(cwt[:, :, 0], conv[:, :, ds(h, 1)].rearrange("p j n -> p (j n)"))
                v.tensor_copy(cwt[:, :, 1], conv[:, :, ds(h + GH, 1)].rearrange("p j n -> p (j n)"))
                v.tensor_copy(cwt[:, :, 2:4], conv[:, :, ds(h * 2 + 2 * GH, 2)])
                settle()
            tap(0)
            if tail:
                dve.wait_ge(vn0_done, i - 1)
                for e in range(2):
                    ins = v.tensor_scalar(vn0[:, e, :], M[:, 3, P * e:P * e + P], bst[:, 0, e:e + 1], None, ALU.mult)
                ins.then_inc(vn0_ready, 1)
            tap(1)
            if hprev:
                dve.wait_ge(hrs_ready, i)
                v.scalar_tensor_tensor(out=hrs, in0=M[:, 1, 0:T], scalar=vec[:, V_HN:V_HN + 1], in1=hrs,
                                       op0=ALU.mult, op1=ALU.mult)
                settle()
                v.tensor_tensor(o_h[:, ds(i - 1, 1), :].rearrange("p n t -> p (n t)"), hrs, hsg, ALU.mult).then_inc(hfin, 1)
            if tail:
                dve.wait_ge(cross_done, i - 1)
                v.tensor_tensor(r1, vsd[:, 1, :, :], M[:, 4, 0:2 * P].rearrange("p (e c) -> p e c", e=2), ALU.subtract
                                ).then_inc(r1_ready, 1)
            tap(2)
            if tail:
                dve.wait_ge(vn1_done, i - 1)
                for e in range(2):
                    ins = v.tensor_scalar(vn1[:, e, :], M[:, 3, T + P * e:T + P * e + P], bst[:, 1, e:e + 1], None, ALU.mult)
                ins.then_inc(vn1_ready, 1)
            tap(3)
            if gemm:
                dve.wait_ge(eh_ready, i + 1)
                v.tensor_scalar(eh, eh, 1e37, None, ALU.min)
                settle()
                v.tensor_scalar(hr, eh, 1.0, None, ALU.add)
                settle()
                v.reciprocal(hr, hr)
                settle()
                v.scalar_tensor_tensor(out=hq, in0=G[:, 1, 0:T], scalar=QSCALE, in1=hr[:, 0:T], op0=ALU.mult, op1=ALU.mult
                                       ).then_inc(evac[1], 1)
                v.scalar_tensor_tensor(out=hk, in0=eh[:, T:2 * T], scalar=lb1[:, ds(i, 1)], in1=hr[:, T:2 * T],
                                       op0=ALU.mult, op1=ALU.mult).then_inc(qk_ready, 1)
                v.tensor_scalar(hf, hr[:, T:2 * T], lb1[:, ds(i, 1)], lb[:, ds(i, 1)], ALU.mult, ALU.add)
                settle()
                v.tensor_scalar(hf, hf, 2.0 ** -63, None, ALU.max).then_inc(f_ready, 1)
            if main:
                dve.wait_ge(ec_ready, i)
                plus_one_inverse(eg)
                v.tensor_tensor(acc.rearrange("p n t -> p (n t)"), acc.rearrange("p n t -> p (n t)"), eg, ALU.mult
                                ).then_inc(act_ready, 1)
                h2 = i * 2 - 2
                v.tensor_copy(bst, beta[:, :, ds(h2, 2)])
                v.tensor_copy(nbst, nbeta[:, :, ds(h2, 2)])
                v.tensor_copy(gst, gam[:, :, ds(h2, 2)])
                v.tensor_copy(gmst, gmx[:, ds(h2, 2)])
                v.tensor_copy(gbc, gdec[:, :, ds(h2, 2)].unsqueeze(3).to_broadcast([P, TT, 2, P])).then_inc(gbc_ready, 1)
                settle()
            if gemm:
                dve.wait_ge(lnf_ready, i + 1)
                for b in range(TT):
                    v.tensor_tensor_scan(hb[:, P * b:P * b + P], ones[:], hf[:, P * b:P * b + P], 0.0, ALU.mult, ALU.add)
                settle()
                middle(1)
                dve.wait_ge(hgx_ready, i + 1)
                v.tensor_copy(hv.rearrange("p i c -> p (i c)"), G[:, 0, 0:T])
                plus_one_inverse(hsg)
                v.tensor_tensor(hsg, hsg, G[:, 0, T:2 * T], ALU.mult).then_inc(evac[0], 1)
            if tail:
                dve.wait_ge(grs_ready, i - 1)
                v.scalar_tensor_tensor(out=zi.rearrange("p i e c -> p (i e c)"), in0=M[:, 5, :], scalar=vec[:, V_GN:V_GN + 1],
                                       in1=xi.rearrange("p i e c -> p (i e c)"), op0=ALU.mult, op1=ALU.mult)
                settle()
                v.tensor_tensor(zi.rearrange("p i e c -> p (i e c)"), zi.rearrange("p i e c -> p (i e c)"),
                                sgz2.rearrange("p e t -> p (e t)"), ALU.mult).then_inc(og_ready, 1)
                dve.wait_ge(ogh_ready, i - 1)
                low_of(xb_lo[:, ds(i * 2 - 4, 2), :].rearrange("p k t -> p (k t)"), zi.rearrange("p i e c -> p (i e c)"),
                       xb_hi[:, ds(i * 2 - 4, 2), :].rearrange("p k t -> p (k t)")).then_inc(ogl_ready, 1)
                settle()
            if main:
                v.tensor_copy(sgz2, sgz).then_inc(sgz_moved, 1)
            scored(0)
            if main:
                dve.wait_ge(gam_done, i)
                for e in range(2):
                    for (b, col, sc) in ((0, 0, gst[:, 0, e:e + 1]), (1, 1, gmst[:, e:e + 1]), (2, 1, gst[:, 1, e:e + 1])):
                        ins = v.tensor_scalar(lt[:, e, P * b:P * b + P], m4(3)[:, col, e, :], sc, 0.0, ALU.subtract, ALU.min)
                ins.then_inc(lt_pre, 1)
            decayed(1)
            middle(2)
            if main:
                dve.wait_ge(rs_ready, i)
                v.tensor_tensor(acc[:, 0:2, :].rearrange("p n t -> p (n t)"), acc[:, 0:2, :].rearrange("p n t -> p (n t)"),
                                eg[:, 2 * T:4 * T], ALU.mult).then_inc(qn_ready, 1)
                dve.wait_ge(lt_ready, i)
                diag = lt.rearrange("p e (b c) -> p e b c", b=3)[:, :, 0:3:2, :]
                v.tensor_tensor(diag, diag, tri[:].unsqueeze(1).unsqueeze(1).to_broadcast([P, 2, 2, P]), ALU.mult)
                settle()
            decayed(2)
            scored(1)
            middle(3)
            if main:
                dve.wait_ge(kq_done, i)
                kk = M[:, 2, 0:3 * P].rearrange("p (b c) -> p b c", b=3)
                for e in range(2):
                    for b in range(TT):
                        v.scalar_tensor_tensor(out=nt[:, b, e, :], in0=kk[:, 2 * b, :], scalar=nbst[:, b, e:e + 1],
                                               in1=lt[:, e, 2 * P * b:2 * P * b + P], op0=ALU.mult, op1=ALU.mult)
                v.tensor_tensor(mt, kk[:, 1, :].unsqueeze(1).to_broadcast([P, 2, P]), lt[:, :, P:T], ALU.mult)
                v.tensor_copy(yi, ident[:].unsqueeze(1).unsqueeze(1).to_broadcast([P, TT, 2, P]))
                settle()
                v.copy_predicated(yi, lmask[:, 0, :].bitcast(I32).unsqueeze(1).unsqueeze(1).to_broadcast([P, TT, 2, P]), nt)
                for e in range(2):
                    v.scalar_tensor_tensor(out=lt[:, e, :], in0=M[:, 5, 0:3 * P], scalar=QSCALE, in1=lt[:, e, :],
                                           op0=ALU.mult, op1=ALU.mult)
                v.drain().then_inc(y0_ready, 1)
            decayed(3)
            scored(2)
            middle(4)
            if gemm:
                chunk_done(2)
                v.tensor_copy(raw[:, 0:2, 4:4 + T], G[:, 1, :].rearrange("p (n t) -> p n t", n=2)).then_inc(evac[1], 1)
            decayed(4)
            scored(3)
            middle(5)
            inverse(1)
            inverse(2)
            if gemm:
                chunk_done(3)
                v.tensor_copy(raw[:, 2:4, 4:4 + T], G[:, 0, :].rearrange("p (n t) -> p n t", n=2)).then_inc(evac[0], 1)
            decayed(5)
            scored(4)
            middle(6)
            inverse(3)
            decayed(6)
            scored(5)
            middle(7)
            inverse(4)
            if gemm:
                dve.wait_ge(evac[1], EV_HEADS[1] + 3 + i * 3)
                plus_one_inverse(gates2[:, ds(i, 1), :, :].rearrange("p n b t -> p (n b t)"))
            decayed(7)
            scored(6)
            middle(8)
            inverse(5)
            decayed(8)
            scored(7)
            inverse(6)
            if gemm:
                dve.wait_ge(gzx_ready, i + 1)
                plus_one_inverse(sgz)
                v.tensor_tensor(sgz, sgz, G[:, 0, :].rearrange("p (e t) -> p e t", e=2), ALU.mult).then_inc(evac[0], 1)
                settle()
            scored(8)

        head(0, True, False, False)
        head(1, True, True, False)
        with dve.Fori(2, GH) as i:
            head(i, True, True, True)
        head(GH, False, True, True)
        head(GH + 1, False, False, True)

        for h in range(2):
            dve.wait_ge(ohh_ready, h + 1)
            low_of(xa_lo[:, 4 * h:4 * h + 4, :].rearrange("p k t -> p (k t)"),
                   o_h[:, 4 * h:4 * h + 4, :].rearrange("p k t -> p (k t)"),
                   xa_hi[:, 4 * h:4 * h + 4, :].rearrange("p k t -> p (k t)")).then_inc(ohl_ready, 1)
        settle()
        for n in range(4):
            dve.wait_ge(gemm_done, FIRST["yh"] + n + 1)
            v.tensor_tensor(o_h[:, 2 * n:2 * n + 2, :], G[:, n % 2, :].rearrange("p (n t) -> p n t", n=2),
                            gates2[:, 2 * n:2 * n + 2, 0, :], ALU.mult).then_inc(evac[n % 2], 1)
        for n in range(8):
            dve.wait_ge(gemm_done, FIRST["yg"] + n + 1)
            v.tensor_tensor(hrs, G[:, n % 2, 0:T], gates2[:, n, 1, :], ALU.mult).then_inc(evac[n % 2], 1)
            settle()
            v.tensor_tensor(o_h[:, n, :], o_h[:, n, :], hrs, ALU.add).then_inc(ym_ready, 1)
            settle()
        for h in range(2):
            dve.wait_ge(ymh_ready, h + 1)
            low_of(xa_lo[:, 4 * h:4 * h + 4, :].rearrange("p k t -> p (k t)"),
                   o_h[:, 4 * h:4 * h + 4, :].rearrange("p k t -> p (k t)"),
                   xa_hi[:, 4 * h:4 * h + 4, :].rearrange("p k t -> p (k t)")).then_inc(yml_ready, 1)
        dve.wait_ge(gemm_done, FIRST["ffn2"])
        residual(1.0, 1.0)
        rms_apply(5)
        gain_low(8, V_FFN2)
        ffn(FIRST["ffn2"], H_FFN2)
        dve.wait_ge(rstd_ready, 6)
        dve.wait_ge(rows_loaded, 32 * 2 + 16)
        for i in range(TT):
            ins = v.scalar_tensor_tensor(out=tmp[:, i, :], in0=res[:, i, :], scalar=stat[:, 44 + i:45 + i], in1=fin_row,
                                         op0=ALU.mult, op1=ALU.mult)
        ins.then_inc(x_normed, 1)

    @block.tensor
    def _(pe):
        mm = nc.tensor.matmul

        def weights_ready(c):
            pe.wait_ge(lo_ready, c + 1)

        def three(out_, w, x, first, last_):
            mm(out_, w[0], x[0], start=first, stop=False)
            mm(out_, w[0], x[1], start=False, stop=False)
            return mm(out_, w[1], x[0], start=False, stop=last_)

        def three_x(out_, x, w, first, last_):
            mm(out_, x[0], w[0], start=first, stop=False)
            mm(out_, x[0], w[1], start=False, stop=False)
            return mm(out_, x[1], w[0], start=False, stop=last_)

        def col_gemm(slot, bank):
            wh, wl = cols(w_hi, slot), cols(w_lo, slot)
            for j in range(2):
                for k in range(KT):
                    ins = three(bank[:, T * j:T * j + T], (wh[:, k, P * j:P * j + P], wl[:, k, P * j:P * j + P]),
                                (xa_hi[:, k, :], xa_lo[:, k, :]), k == 0, k == KT - 1)
            ins.then_inc(gemm_done, 1)

        def tok_gemm(slot, bank):
            wh, wl = cols(w_hi, slot), cols(w_lo, slot)
            for i in range(TT):
                for k in range(KT):
                    ins = three_x(bank[:, CW * i:CW * i + CW],
                                  (xa_hi[:, k, P * i:P * i + P], xa_lo[:, k, P * i:P * i + P]),
                                  (wh[:, k, :], wl[:, k, :]), k == 0, k == KT - 1)
            ins.then_inc(gemm_done, 1)

        def row_gemm(slot, xh, xl, first, last_):
            wh, wl = rows2(w_hi, slot), rows2(w_lo, slot)
            for k in range(2):
                for i in range(TT):
                    for h in range(2):
                        ins = three_x(M[:, 2 * i + h, :], (xh[:, k, P * i:P * i + P], xl[:, k, P * i:P * i + P]),
                                      (wh[:, k, 512 * h:512 * h + 512], wl[:, k, 512 * h:512 * h + 512]),
                                      first and k == 0, last_ and k == 1)
            ins.then_inc(gemm_done, 1)

        def transposed(src):
            for h in range(2):
                for k in range(4 * h, 4 * h + 4):
                    for i in range(TT):
                        at = (k % 2) * T + P * i
                        ins = nc.tensor.transpose(M[:, k // 2, at:at + P], src[:, i, P * k:P * k + P], ident[:])
                ins.then_inc(xt_done, 1)

        pe.wait_ge(x_loaded, 16 * TT)
        pe.wait_ge(built, BUILT_ID)
        transposed(res)
        pe.wait_ge(xl_ready, 2)
        weights_ready(0)
        wh, wl = cols(w_hi, 0), cols(w_lo, 0)
        for k in range(KT):
            three(G[:, 0, 0:T], (wh[:, k, 0:P], wl[:, k, 0:P]), (xa_hi[:, k, :], xa_lo[:, k, :]), k == 0, k == KT - 1)
        for i in range(TT):
            for k in range(KT):
                ins = three_x(G[:, 0, T + 24 * i:T + 24 * i + 24],
                              (xa_hi[:, k, P * i:P * i + P], xa_lo[:, k, P * i:P * i + P]),
                              (wh[:, k, P:P + 24], wl[:, k, P:P + 24]), k == 0, k == KT - 1)
        ins.then_inc(gemm_done, 1)

        def bank_free(c):
            if c >= 2:
                pe.wait_ge(evac[c % 2], c // 2)

        def static_chunk(c, gemm):
            weights_ready(c)
            bank_free(c)
            gemm(c % RING, G[:, c % 2, :])

        def dots(u):
            c = FIRST["qi"] + u
            pe.wait_ge(evac[c % 2], c // 2 + 1)
            if u >= 1:
                pe.wait_ge(relu_ready, u)
            for e in range(4):
                lo_ = HD * (e % 2)
                q = qi_t[lo_:lo_ + HD, u % 2, T * (e // 2):T * (e // 2) + T]
                k = ki_t[lo_:lo_ + HD, :]
                mm(M[:, e, 0:P], q[:, 0:P], k[:, 0:P], start=True, stop=True)
                ins = mm(M[:, e, P:3 * P], q[:, P:T], k, start=True, stop=True)
            ins.then_inc(dots_done, 1)

        static_chunk(1, col_gemm)
        static_chunk(2, col_gemm)
        dots(0)
        pe.wait_ge(logf_ready, 1)
        pe.wait_ge(built, BUILT_MASKS)
        mm(M[:, 5, 0:NH], tri[:], log_f[:, 0, :], start=True, stop=True)
        mm(M[:, 5, NH:2 * NH], ones[:], log_f[:, 0, :], start=True, stop=False)
        mm(M[:, 5, NH:2 * NH], tri[:], log_f[:, 1, :], start=False, stop=True).then_inc(cum_done, 1)
        static_chunk(3, col_gemm)
        dots(1)
        static_chunk(4, col_gemm)
        dots(2)
        static_chunk(5, tok_gemm)
        dots(3)
        static_chunk(6, tok_gemm)
        for c in range(FIRST["gates"], FIRST["pairs"]):
            static_chunk(c, col_gemm)

        c0 = FIRST["pairs"]
        pe.wait_ge(relu_ready, 4)
        pe.wait_ge(c_ready, 1)

        def pair_chunk(j, p, gemm):
            weights_ready(c0 + j + p * 6)
            pe.wait_ge(evac[(c0 + j) % 2], (c0 + j) // 2 + p * 3)
            gemm((c0 + j) % RING, G[:, (c0 + j) % 2, :])

        def copied(j, p):
            pe.wait_ge(evac[(c0 + j) % 2], (c0 + j) // 2 + 1 + p * 3)

        def scores(n, bank, q, k, p):
            for e in range(2):
                lo_ = HD * e
                mm(M[:, bank + e, 0:P], q[lo_:lo_ + HD, 0:P], k[lo_:lo_ + HD, 0:P], start=True, stop=True)
                ins = mm(M[:, bank + e, P:3 * P], q[lo_:lo_ + HD, P:T], k[lo_:lo_ + HD, :], start=True, stop=True)
            ins.then_inc(sc_done[n], 1)

        def prob_t(n, bank, lg, p):
            pe.wait_ge(prob_ready[n], p + 1)
            for e in range(2):
                for b in range(3):
                    ins = nc.tensor.transpose(M[:, bank + e, P * b:P * b + P], lg[:, e, P * b:P * b + P], ident[:])
            ins.then_inc(pt_done[n], 1)

        def values(n, bank, v0, v1, pt):
            for e in range(2):
                o = M[HD * e:HD * e + HD, bank, 0:T]
                mm(o, v0[:, HD * e:HD * e + HD], pt[:, e, 0:T], start=True, stop=False)
                ins = mm(o[:, P:T], v1[:, HD * e:HD * e + HD], pt[:, e, T:3 * P], start=False, stop=True)
            ins.then_inc(o_done[n], 1)

        with pe.Fori(0, PAIRS) as p:
            pair_chunk(0, p, col_gemm)
            pair_chunk(1, p, col_gemm)
            copied(0, p)
            for e in range(2):
                lo_ = HD * e
                mm(M[:, 4 + e, 0:T], ks_t[lo_:lo_ + HD, 0:P], qs_t[lo_:lo_ + HD, :], start=True, stop=True)
                ins = mm(M[:, 4 + e, T:3 * P], ks_t[lo_:lo_ + HD, P:T], qs_t[lo_:lo_ + HD, P:T], start=True, stop=True)
            ins.then_inc(z_done, 1)
            pe.wait_ge(fbc_ready, p + 1)
            for e in range(2):
                mm(M[:, 2 + e, 0:P], fbc[:, 0, e, :], tri[:], start=True, stop=True)
                mm(M[:, 2 + e, P:T], fbc[:, 0, e, :], ones[:], start=True, stop=False)
                ins = mm(M[:, 2 + e, P:T], fbc[:, 1, e, :], tri[:], start=False, stop=True)
            ins.then_inc(ck_done, 1)
            pair_chunk(2, p, col_gemm)
            copied(1, p)
            scores(0, 0, qa_t, ka_t, p)
            pair_chunk(3, p, tok_gemm)
            pe.wait_ge(lom_ready, p + 1)
            for e in range(2):
                mm(M[:, 4 + e, 0:T], below[:], st3[:, e, 0:T], start=True, stop=False)
                mm(M[:, 4 + e, P:T], ones[:], st3[:, e, T:3 * P], start=False, stop=True)
                ins = mm(M[:, 4 + e, T:3 * P], below[:], st3[:, e, T:3 * P], start=True, stop=True)
            ins.then_inc(later_done, 1)
            copied(2, p)
            pe.wait_ge(mck_ready, p + 1)
            scores(1, 2, qf_t, kf_t, p)
            prob_t(0, 0, log_a, p)
            pair_chunk(4, p, col_gemm)
            pe.wait_ge(stick_ready, p + 1)
            copied(3, p)
            values(2, 4, vfs[:, 0, P:T], vfs[:, 1, P:T], st2)
            pe.wait_ge(pt_ready[0], p + 1)
            pe.wait_ge(va_ready, p + 1)
            values(0, 0, va_p[:, 0, :], va_p[:, 1, :], pt_a)
            prob_t(1, 2, log_fo, p)
            pair_chunk(5, p, col_gemm)
            pe.wait_ge(pt_ready[1], p + 1)
            values(1, 2, vfs[:, 0, 0:P], vfs[:, 1, 0:P], pt_f)
            for n in range(3):
                pe.wait_ge(ol_ready[n], p + 1)

        c0 = FIRST["branch"]
        for n in range(6):
            i, slot = n % 3, (c0 + n) % RING
            weights_ready(c0 + n)
            if n >= 3:
                pe.wait_ge(branch_used, n - 2)
            wh = w_hi[:, slot, :].rearrange("p (k c) -> p k c", c=512)
            wl = w_lo[:, slot, :].rearrange("p (k c) -> p k c", c=512)
            for j in range(4):
                for k in range(4):
                    ins = three(M[:, 2 * i + j // 2, T * (j % 2):T * (j % 2) + T],
                                (wh[:, k, P * j:P * j + P], wl[:, k, P * j:P * j + P]),
                                (xb_hi[:, 4 * i + k, :], xb_lo[:, 4 * i + k, :]), k == 0, k == 3)
            ins.then_inc(gemm_done, 1)
        c0 = FIRST["wout"]
        pe.wait_ge(branch_used, 6)
        for u in range(4):
            weights_ready(c0 + u)
            pe.wait_ge(ml_ready, 1 + u // 2)
            row_gemm((c0 + u) % RING, xa_hi[:, 2 * u:2 * u + 2, :], xa_lo[:, 2 * u:2 * u + 2, :], u == 0, u == 3)
        pe.wait_ge(x_normed, 1)
        transposed(res)
        pe.wait_ge(vecs_loaded, 16 * 9)
        nc.tensor.transpose(M[:, 4, 0:VECS], vec_rows[0:VECS, :], ident[0:VECS, 0:VECS])
        nc.tensor.transpose(M[:, 4, P:2 * P], conv_rows, ident[:]).then_inc(vec_done, 1)
        pe.wait_ge(xl_ready, 4)

        def ff1(c, slot, r, turn):
            weights_ready(c)
            if r < 2:
                pe.wait_ge(evac[r], EV_FF[r] + turn)
            col_gemm(slot, ffbank(r))

        def ff2(c, slot, g, r, first, last_):
            weights_ready(c)
            pe.wait_ge(h_ready, g + 1)
            row_gemm(slot, xb_hi[:, 2 * r:2 * r + 2, :], xb_lo[:, 2 * r:2 * r + 2, :], first, last_)

        c0 = FIRST["ff"]
        ff1(c0, c0 % RING, 0, 0)

        def ff_steps(i, first):
            for u in range(3):
                c = c0 + 1 + 2 * u
                ff1(c + i * 6, c % RING, (1 + u) % 3, (1 + u) // 3 + i)
                ff2(c + 1 + i * 6, (c + 1) % RING, u + i * 3, u, first and u == 0, False)

        ff_steps(0, True)
        with pe.Fori(1, 5) as i:
            ff_steps(i, False)
        c = c0 + 31
        ff2(c, c % RING, 15, 0, False, True)
        def ffn(c0, ev, h0):
            def up(c, i, step, n, turn):
                weights_ready(c + i * step)
                pe.wait_ge(evac[n], ev[n] + turn)
                col_gemm(c % RING, G[:, n, :])

            def down(c, i, step, r, g, first, last_):
                weights_ready(c + i * step)
                pe.wait_ge(h_ready, h0 + 2 * g + 2)
                row_gemm(c % RING, xb_hi[:, 2 * r:2 * r + 2, :], xb_lo[:, 2 * r:2 * r + 2, :], first, last_)

            def steps(i, first):
                for u in range(2):
                    c = c0 + 2 + 3 * u
                    for n in range(2):
                        up(c + n, i, 6, n, 1 + u + i * 2)
                    down(c + 2, i, 6, u, u + i * 2, first and u == 0, False)

            for n in range(2):
                up(c0 + n, 0, 0, n, 0)
            steps(0, True)
            with pe.Fori(1, 5) as i:
                steps(i, False)
            down(c0 + 32, 0, 0, 0, 10, False, True)

        pe.wait_ge(x_normed, 3)
        transposed(tmp)
        pe.wait_ge(xl_ready, 6)
        ffn(FIRST["ffn1"], EV_FFN1, H_FFN1)
        pe.wait_ge(x_normed, 4)
        transposed(tmp)
        pe.wait_ge(xl_ready, 8)
        c = FIRST["ba"]
        weights_ready(c)
        pe.wait_ge(evac[0], EV_BA)
        wh, wl_ = cols(w_hi, c % RING), cols(w_lo, c % RING)
        for i in range(TT):
            for k in range(KT):
                ins = three_x(G[:, 0, 2 * VH * i:2 * VH * i + 2 * VH],
                              (xa_hi[:, k, P * i:P * i + P], xa_lo[:, k, P * i:P * i + P]),
                              (wh[:, k, 0:2 * VH], wl_[:, k, 0:2 * VH]), k == 0, k == KT - 1)
        ins.then_inc(gemm_done, 1)
        pe.wait_ge(g_ready, 1)
        for b in range(TT):
            mm(M[:, 4, VH * b:VH * b + VH], tri[:], gdec[:, b, :], start=True, stop=True)
        mm(M[:, 4, 2 * VH:3 * VH], ones[:], gdec[:, 0, :], start=True, stop=True).then_inc(gsum_done, 1)

        c0 = FIRST["heads"]

        def head(i, gemm, main, tail):
            hprev = not isinstance(i, int) or 1 <= i <= GH

            def quarter(j, n):
                if not gemm:
                    return
                slot, bank = (c0 + j) % RING, (j + 1) % 2
                if n == 0:
                    weights_ready(c0 + j + i * 6)
                    pe.wait_ge(evac[bank], EV_HEADS[bank] + j // 2 + i * 3)
                wh, wl_ = cols(w_hi, slot), cols(w_lo, slot)
                if j == 1 and n < 2:
                    for k in range(KT):
                        ins = three_x(G[:, bank, P * n:P * n + P], (xa_hi[:, k, P * n:P * n + P], xa_lo[:, k, P * n:P * n + P]),
                                      (wh[:, k, 0:P], wl_[:, k, 0:P]), k == 0, k == KT - 1)
                else:
                    t = n // 2
                    for k in range(4 * (n % 2), 4 * (n % 2) + 4):
                        ins = three(G[:, bank, T * t:T * t + T], (wh[:, k, P * t:P * t + P], wl_[:, k, P * t:P * t + P]),
                                    (xa_hi[:, k, :], xa_lo[:, k, :]), k == 0, k == KT - 1)
                if n == 3:
                    ins.then_inc(gemm_done, 1)

            def level(l):
                if not gemm:
                    return
                if l == 0:
                    pe.wait_ge(qk_ready, i + 1)
                    after(pe, sc_used, i * 9)
                    left, right = hk, hq
                else:
                    pe.wait_ge(wl_ready, l + i * 8)
                    pe.wait_ge(sc_used, l + i * 9)
                    left = right = kqd[:, l % 2, :]
                at = T * (l % 2)
                if l == 8:
                    mm(M[:, 0, at:at + P], left[:, 0:P], right[:, P:T], start=True, stop=True).then_inc(lev_done, 1)
                    return
                for b in range(TT):
                    ins = mm(M[:, 0, at + P * b:at + P * b + P], left[:, P * b:P * b + P], right[:, P * b:P * b + P],
                             start=True, stop=True)
                ins.then_inc(lev_done, 1)

            def four(out_bank, lhs, rhs, done):
                for b in range(TT):
                    for e in range(2):
                        at = T * b + P * e
                        ins = mm(M[:, out_bank, at:at + P], lhs[:, b, e, :], rhs[:, b, e, :], start=True, stop=True)
                ins.then_inc(done, 1)

            def inv_t(src, t):
                if not main:
                    return
                if t == 0:
                    pe.wait_ge(y0_ready, i)
                else:
                    pe.wait_ge(xx_ready, t + (i - 1) * 6)
                for b in range(TT):
                    for e in range(2):
                        at = T * b + P * e
                        ins = nc.tensor.transpose(M[:, 5, at:at + P], src[:, b, e, :], ident[:])
                ins.then_inc(t_done, 1)

            def inv_z(l):
                if not main:
                    return
                if l == 1:
                    pe.wait_ge(t_ready, 1 + (i - 1) * 7)
                else:
                    pe.wait_ge(xx_ready, l - 1 + (i - 1) * 6)
                four(3, nt, xi, zz_done)

            def inv_w(l):
                if not main:
                    return
                pe.wait_ge(zc_ready, l + (i - 1) * 6)
                pe.wait_ge(t_ready, l + (i - 1) * 7)
                four(4, yi, zi, ww_done)

            quarter(0, 0)
            if hprev:
                pe.wait_ge(sc_used, i * 9)
                after(pe, hfin, i - 1)
                pe.wait_ge(evac[0], EV_HEADS[0] + 1 + (i - 1) * 3)
                mm(M[:, 1, 0:P], hv[:, 0, :], sct[:, 0:P], start=True, stop=True)
                mm(M[:, 1, P:T], hv[:, 1, :], sct[:, P:T], start=True, stop=False)
                mm(M[:, 1, P:T], hv[:, 0, :], sct[:, T:3 * P], start=False, stop=True).then_inc(hpv_done, 1)
            quarter(0, 1)
            if tail:
                pe.wait_ge(t_ready, (i - 1) * 7)
                for e in range(2):
                    ins = mm(M[:, 3, P * e:P * e + P], yi[:, 0, e, :], vsd[:, 0, e, :], start=True, stop=True)
                ins.then_inc(vn0_done, 1)
            quarter(0, 2)
            if hprev:
                pe.wait_ge(hsq_ready, i)
                mm(M[:, 1, T:2 * T], ones[:], hsq, start=True, stop=True).then_inc(hss_done, 1)
            if tail:
                pe.wait_ge(vn0_ready, i - 1)
                for e in range(2):
                    ins = mm(M[:, 4, P * e:P * e + P], mt[:, e, :], vn0[:, e, :], start=True, stop=True)
                ins.then_inc(cross_done, 1)
            quarter(0, 3)
            if tail:
                pe.wait_ge(r1_ready, i - 1)
                for e in range(2):
                    ins = mm(M[:, 3, T + P * e:T + P * e + P], yi[:, 1, e, :], r1[:, e, :], start=True, stop=True)
                ins.then_inc(vn1_done, 1)
            quarter(1, 0)
            if tail:
                pe.wait_ge(vn1_ready, i - 1)
                for e in range(2):
                    o = M[:, 5, T * e:T * e + T]
                    mm(o, vn0[:, e, :], lt[:, e, 0:T], start=True, stop=False)
                    ins = mm(o[:, P:T], vn1[:, e, :], lt[:, e, T:3 * P], start=False, stop=True)
                ins.then_inc(go_done, 1)
            quarter(1, 1)
            if tail:
                pe.wait_ge(gsq_ready, i - 1)
                mm(M[:, 2, :], ones[:], zi.rearrange("p i e c -> p (i e c)"), start=True, stop=True).then_inc(gss_done, 1)
            quarter(1, 2)
            level(0)
            quarter(1, 3)
            if main:
                if tail:
                    pe.wait_ge(og_ready, i - 1)
                pe.wait_ge(sq_ready, i)
                mm(M[:, 5, :], ones[:], eg[:, 0:2 * T], start=True, stop=True).then_inc(ss_done, 1)
                for b in range(TT):
                    for e in range(2):
                        ins = nc.tensor.transpose(M[:, 4, T * b + P * e:T * b + P * e + P], acc[:, 2 + e, P * b:P * b + P],
                                                  ident[:])
                ins.then_inc(vt_done, 1)
                pe.wait_ge(gbc_ready, i)
                for b in range(TT):
                    for e in range(2):
                        ins = mm(M[:, 3, T * b + P * e:T * b + P * e + P], gbc[:, b, e, :], tri[:], start=True, stop=True)
                ins.then_inc(gam_done, 1)
            quarter(2, 0)
            level(1)
            quarter(2, 1)
            if main:
                pe.wait_ge(qn_ready, i)
                for bank, x in ((2, acc[:, 1, :]), (5, acc[:, 0, :])):
                    mm(M[:, bank, 0:T], acc[:, 1, 0:P], x, start=True, stop=True)
                    ins = mm(M[:, bank, T:3 * P], acc[:, 1, P:T], x[:, P:T], start=True, stop=True)
                ins.then_inc(kq_done, 1)
            level(2)
            quarter(2, 2)
            inv_t(yi, 0)
            quarter(2, 3)
            inv_z(1)
            level(3)
            quarter(3, 0)
            inv_w(1)
            quarter(3, 1)
            inv_t(xi, 1)
            inv_z(2)
            quarter(3, 2)
            inv_w(2)
            level(4)
            quarter(3, 3)
            inv_t(xi, 2)
            inv_z(3)
            quarter(4, 0)
            inv_w(3)
            quarter(4, 1)
            inv_t(xi, 3)
            inv_z(4)
            level(5)
            quarter(4, 2)
            inv_w(4)
            quarter(4, 3)
            inv_t(xi, 4)
            inv_z(5)
            level(6)
            quarter(5, 0)
            inv_w(5)
            quarter(5, 1)
            inv_t(xi, 5)
            inv_z(6)
            level(7)
            quarter(5, 2)
            inv_w(6)
            quarter(5, 3)
            inv_t(xi, 6)
            level(8)

        head(0, True, False, False)
        head(1, True, True, False)
        with pe.Fori(2, GH) as i:
            head(i, True, True, True)
        head(GH, False, True, True)
        head(GH + 1, False, False, True)

        pe.wait_ge(ohl_ready, 2)
        for n in range(4):
            c = FIRST["yh"] + n
            weights_ready(c)
            pe.wait_ge(evac[n % 2], EV_Y[n % 2] + n // 2)
            col_gemm(c % RING, G[:, n % 2, :])
        pe.wait_ge(ogl_ready, GH)
        for n in range(8):
            c = FIRST["yg"] + n
            weights_ready(c)
            pe.wait_ge(evac[n % 2], EV_Y[n % 2] + 2 + n // 2)
            wh = w_hi[:, c % RING, :].rearrange("p (k c) -> p k c", c=P)
            wl_ = w_lo[:, c % RING, :].rearrange("p (k c) -> p k c", c=P)
            for k in range(16):
                ins = three(G[:, n % 2, 0:T], (wh[:, k, :], wl_[:, k, :]), (xb_hi[:, k, :], xb_lo[:, k, :]),
                            k == 0, k == 15)
            ins.then_inc(gemm_done, 1)
        for u in range(4):
            c = FIRST["wout2"] + u
            weights_ready(c)
            pe.wait_ge(yml_ready, 1 + u // 2)
            row_gemm(c % RING, xa_hi[:, 2 * u:2 * u + 2, :], xa_lo[:, 2 * u:2 * u + 2, :], u == 0, u == 3)
        pe.wait_ge(x_normed, 5)
        transposed(tmp)
        pe.wait_ge(xl_ready, 10)
        ffn(FIRST["ffn2"], EV_FFN2, H_FFN2)


_INS = (
    "x", "w_in", "b_forget", "w_branch", "w_out", "ln1_g",
    "ln1_b", "w_ff1", "w_ff2", "ln2_g", "ln2_b", "ffn1_norm_2",
    "ffn1_w_in_2", "ffn1_w_out_2", "mix_norm_2", "w_in_2", "hgrn_lb_logits_2", "hgrn_out_norm_2",
    "gdn_conv_w_2", "gdn_a_log_2", "gdn_dt_bias_2", "gdn_out_norm_2", "w_branch_hgrn_2", "w_branch_gdn_2",
    "w_out_2", "ffn2_norm_2", "ffn2_w_in_2", "ffn2_w_out_2", "final_norm_2",
)


def kernel(**inputs):
    import numpy as _np
    import concourse.bacc as _bacc
    from concourse.bass_utils import run_bass_kernel_spmd as _run

    nc = _bacc.Bacc("TRN2", target_bir_lowering=False, num_devices=1)
    arrays, aps = {}, {}
    for name in _INS:
        arrays[f"in_{name}"] = _np.ascontiguousarray(inputs[name])
        aps[name] = nc.dram_tensor(f"in_{name}", arrays[f"in_{name}"].shape, F32, kind="ExternalInput").ap()
    out = nc.dram_tensor("out_0", (1, T, D), F32, kind="ExternalOutput").ap()
    build_program(nc, aps, out)
    r = _run(nc, [arrays], core_ids=[0])
    return r.results[0]["out_0"]
```
